# Optimizing a Trainium2 kernel written in Bass

```python
import jax, jax.numpy as jnp
from jax import lax
import numpy as np
import math

D_MODEL = 1024
BATCH = 1
SEQ = 256
DEPTH = 2

D_MIX = D_MODEL
RET_HEADS = 4
RET_HEAD_DIM = 128
RET_WIDTH = RET_HEADS * RET_HEAD_DIM
RET_CHUNK = 128
GDN_HEADS = 4
GDN_HEAD_DIM = 128
GDN_WIDTH = GDN_HEADS * GDN_HEAD_DIM
GDN_CHUNK = 64
CONV_K = 5
D_FF = 2816
MEM_LEN = 256
XATTN_HEADS = 4
XATTN_HEAD_DIM = D_MODEL // XATTN_HEADS
ROPE_BASE = 10000.0
NORM_EPS = 1e-6
N_SUBLAYERS = 4
IN_COLS = 4 * RET_WIDTH + 4 * GDN_WIDTH + 4 * GDN_HEADS
IN_SPLITS = (RET_WIDTH, 2 * RET_WIDTH, 3 * RET_WIDTH, 4 * RET_WIDTH,
             4 * RET_WIDTH + 3 * GDN_WIDTH, 4 * RET_WIDTH + 4 * GDN_WIDTH,
             4 * RET_WIDTH + 4 * GDN_WIDTH + 2 * GDN_HEADS)


def rms_norm(x, w):
    xf = x.astype(jnp.float32)
    y = xf * lax.rsqrt(jnp.mean(xf * xf, axis=-1, keepdims=True) + NORM_EPS)
    return (y * w.astype(jnp.float32)).astype(x.dtype)

def swiglu(u, w_gate, w_up, w_down):
    return (jax.nn.silu(u @ w_gate) * (u @ w_up)) @ w_down

def rotary_tables(positions):
    inv_freq = ROPE_BASE ** (-jnp.arange(0, RET_HEAD_DIM, 2, dtype=jnp.float32) / RET_HEAD_DIM)
    ang = positions.astype(jnp.float32)[..., None] * inv_freq
    return jnp.cos(ang)[:, :, None, :], jnp.sin(ang)[:, :, None, :]

def rotary(x, cos, sin):
    half = x.shape[-1] // 2
    x1, x2 = x[..., :half], x[..., half:]
    return jnp.concatenate([x1 * cos - x2 * sin, x1 * sin + x2 * cos], axis=-1)

def flip_seq(t):
    return jnp.flip(t, axis=2)

def retention_direction(q, k, v, log_gamma, strict):
    b, h, s, d = q.shape
    n = s // RET_CHUNK
    q, k, v = (t.reshape(b, h, n, RET_CHUNK, d) for t in (q, k, v))
    pos = jnp.arange(RET_CHUNK, dtype=jnp.float32)
    rel = pos[:, None] - pos[None, :]
    mask = rel > 0 if strict else rel >= 0
    lg = log_gamma[:, None, None]
    dmat = jnp.where(mask, jnp.exp(jnp.where(mask, rel, 0.0) * lg), 0.0)
    scores = jnp.einsum('bhnid,bhnjd->bhnij', q, k) * dmat[:, None]
    o_intra = jnp.einsum('bhnij,bhnje->bhnie', scores, v)
    lgv = log_gamma[:, None]
    k_dec = k * jnp.exp((RET_CHUNK - 1.0 - pos) * lgv)[:, None, :, None]
    chunk_kv = jnp.einsum('bhncd,bhnce->bhnde', k_dec, v)
    chunk_decay = jnp.exp(RET_CHUNK * log_gamma)[None, :, None, None]

    def step(state, kv_c):
        return state * chunk_decay + kv_c, state

    _, prev = lax.scan(step, jnp.zeros((b, h, d, d), q.dtype), jnp.moveaxis(chunk_kv, 2, 0))
    prev = jnp.moveaxis(prev, 0, 2)
    q_dec = q * jnp.exp((pos + 1.0) * lgv)[:, None, :, None]
    o_inter = jnp.einsum('bhncd,bhnde->bhnce', q_dec, prev)
    return (o_intra + o_inter).reshape(b, h, s, d)

def retention_group(rq, rk, rv, rg, cos, sin, log_gamma):
    b, s, _ = rq.shape
    heads = lambda t: t.reshape(b, s, RET_HEADS, RET_HEAD_DIM)
    q = rotary(heads(rq), cos, sin)
    k = rotary(heads(rk), cos, sin) * RET_HEAD_DIM ** -0.5
    v = heads(rv)
    q, k, v = (jnp.swapaxes(t, 1, 2).astype(jnp.float32) for t in (q, k, v))
    lgam = log_gamma.astype(jnp.float32)
    fwd = retention_direction(q, k, v, lgam[0], strict=False)
    bwd = retention_direction(flip_seq(q), flip_seq(k), flip_seq(v), lgam[1], strict=True)
    o = fwd + flip_seq(bwd)
    mu = jnp.mean(o, axis=-1, keepdims=True)
    var = jnp.mean(jnp.square(o - mu), axis=-1, keepdims=True)
    o = (o - mu) * lax.rsqrt(var + NORM_EPS)
    o = jnp.swapaxes(o, 1, 2).reshape(b, s, RET_WIDTH).astype(rg.dtype)
    return jax.nn.silu(rg) * o

def gdn_direction(q, k, v, g, beta):
    b, h, s, dk = q.shape
    dv = v.shape[-1]
    n = s // GDN_CHUNK
    c = GDN_CHUNK
    q, k, v = (t.reshape(b, h, n, c, t.shape[-1]) for t in (q, k, v))
    g = jnp.cumsum(g.reshape(b, h, n, c), axis=-1)
    beta = beta.reshape(b, h, n, c)
    tril = jnp.tril(jnp.ones((c, c), bool))
    strict = jnp.tril(jnp.ones((c, c), bool), -1)
    decay = jnp.exp(jnp.where(tril, g[..., :, None] - g[..., None, :], -jnp.inf))
    k_beta = k * beta[..., None]
    lower = jnp.where(strict, jnp.einsum('bhnid,bhnjd->bhnij', k_beta, k) * decay, 0.0)
    rhs = jnp.concatenate([v * beta[..., None], k_beta * jnp.exp(g)[..., None]], axis=-1)
    sol = lax.linalg.triangular_solve(lower, rhs, left_side=True, lower=True, unit_diagonal=True)
    u, w = sol[..., :dv], sol[..., dv:]
    qk = jnp.einsum('bhnid,bhnjd->bhnij', q, k) * decay
    q_g = q * jnp.exp(g)[..., None]
    k_tail = k * jnp.exp(g[..., -1:] - g)[..., None]
    g_last = jnp.exp(g[..., -1])

    def step(state, xs):
        u_c, w_c, qk_c, qg_c, kt_c, gl_c = xs
        v_new = u_c - w_c @ state
        o_c = qg_c @ state + qk_c @ v_new
        state = state * gl_c[..., None, None] + jnp.swapaxes(kt_c, -1, -2) @ v_new
        return state, o_c

    xs = tuple(jnp.moveaxis(t, 2, 0) for t in (u, w, qk, q_g, k_tail, g_last))
    _, o = lax.scan(step, jnp.zeros((b, h, dk, dv), jnp.float32), xs)
    return jnp.moveaxis(o, 0, 2).reshape(b, h, s, dv)

def centred_depthwise_conv(x, w):
    return lax.conv_general_dilated(
        x, w[:, None, :], window_strides=(1,),
        padding=[((CONV_K - 1) // 2, CONV_K // 2)],
        dimension_numbers=('NWC', 'WIO', 'NWC'),
        feature_group_count=x.shape[-1])

def gdn_group(qkv, z, a, bl, conv_w, a_log, dt_bias, norm_w):
    b, s, _ = qkv.shape
    qkv = jax.nn.silu(centred_depthwise_conv(qkv, conv_w))
    q, k, v = jnp.split(qkv, 3, axis=-1)
    heads = lambda t: jnp.swapaxes(t.reshape(b, s, GDN_HEADS, GDN_HEAD_DIM), 1, 2).astype(jnp.float32)
    q, k, v = heads(q), heads(k), heads(v)
    l2n = lambda t: t * lax.rsqrt(jnp.sum(t * t, axis=-1, keepdims=True) + NORM_EPS)
    q = l2n(q) * GDN_HEAD_DIM ** -0.5
    k = l2n(k)
    dir_heads = lambda t: jnp.transpose(t.reshape(b, s, 2, GDN_HEADS), (2, 0, 3, 1)).astype(jnp.float32)
    a, bl = dir_heads(a), dir_heads(bl)
    g = -jnp.exp(a_log.astype(jnp.float32))[:, None, :, None] * jax.nn.softplus(
        a + dt_bias.astype(jnp.float32)[:, None, :, None])
    beta = jax.nn.sigmoid(bl)
    fwd = gdn_direction(q, k, v, g[0], beta[0])
    bwd = gdn_direction(flip_seq(q), flip_seq(k), flip_seq(v), flip_seq(g[1]), flip_seq(beta[1]))
    o = fwd + flip_seq(bwd)
    o = o * lax.rsqrt(jnp.mean(o * o, axis=-1, keepdims=True) + NORM_EPS) * norm_w.astype(jnp.float32)
    o = jnp.swapaxes(o, 1, 2).reshape(b, s, GDN_WIDTH).astype(z.dtype)
    return o * jax.nn.silu(z)

def parallel_head_groups(u, cos, sin, w_in, conv_w, ret_log_gamma, a_log, dt_bias, gdn_norm_w, w_out):
    proj = u @ w_in
    rq, rk, rv, rg, qkv, z, a, bl = jnp.split(proj, IN_SPLITS, axis=-1)
    o_ret = retention_group(rq, rk, rv, rg, cos, sin, ret_log_gamma)
    o_gdn = gdn_group(qkv, z, a, bl, conv_w, a_log, dt_bias, gdn_norm_w)
    return jnp.concatenate([o_ret, o_gdn], axis=-1) @ w_out

def memory_cross_attention(u, mem_n, wq, wk, wv, wo):
    b, s, _ = u.shape
    m = mem_n.shape[1]
    q = (u @ wq).reshape(b, s, XATTN_HEADS, XATTN_HEAD_DIM)
    k = (mem_n @ wk).reshape(b, m, XATTN_HEADS, XATTN_HEAD_DIM)
    v = (mem_n @ wv).reshape(b, m, XATTN_HEADS, XATTN_HEAD_DIM)
    scores = jnp.einsum('bshd,bmhd->bhsm', q, k).astype(jnp.float32) * XATTN_HEAD_DIM ** -0.5
    p = jax.nn.softmax(scores, axis=-1).astype(v.dtype)
    o = jnp.einsum('bhsm,bmhd->bshd', p, v).reshape(b, s, D_MODEL)
    return o @ wo

def first_inputs(seed: int = 0) -> dict:
    key = jax.random.key(seed)
    ks = jax.random.split(key, 24)
    nrm = lambda k, shape: jax.random.normal(k, shape, jnp.float32)
    dense = lambda k, shape, fan_in: nrm(k, shape) * fan_in ** -0.5
    gain = lambda k, shape: 1.0 + 0.02 * nrm(k, shape)
    x = nrm(ks[0], (BATCH, SEQ, D_MODEL))
    mem = nrm(ks[1], (BATCH, MEM_LEN, D_MODEL))
    positions = jnp.broadcast_to(jnp.arange(SEQ, dtype=jnp.int32)[None, :], (BATCH, SEQ))
    base = jnp.log1p(-(2.0 ** (-5.0 - jnp.arange(RET_HEADS, dtype=jnp.float32))))
    ret_log_gamma = base * (1.0 + 0.05 * nrm(ks[10], (DEPTH, 2, RET_HEADS)))
    gdn_a_log = jnp.log(jax.random.uniform(ks[11], (DEPTH, 2, GDN_HEADS), jnp.float32, 1.0, 16.0))
    dt = jnp.exp(jax.random.uniform(ks[12], (DEPTH, 2, GDN_HEADS), jnp.float32,
                                    float(np.log(1e-3)), float(np.log(1e-1))))
    gdn_dt_bias = dt + jnp.log(-jnp.expm1(-dt))
    return {
        "x": x,
        "mem": mem,
        "positions": positions,
        "norm_pre": gain(ks[2], (DEPTH, N_SUBLAYERS, D_MODEL)),
        "norm_post": gain(ks[3], (DEPTH, N_SUBLAYERS, D_MODEL)),
        "mem_norm": gain(ks[4], (DEPTH, D_MODEL)),
        "ffn1_gate": dense(ks[5], (DEPTH, D_MODEL, D_FF), D_MODEL),
        "ffn1_up": dense(ks[6], (DEPTH, D_MODEL, D_FF), D_MODEL),
        "ffn1_down": dense(ks[7], (DEPTH, D_FF, D_MODEL), D_FF),
        "w_in": dense(ks[8], (DEPTH, D_MODEL, IN_COLS), D_MODEL),
        "gdn_conv": dense(ks[9], (DEPTH, CONV_K, 3 * GDN_WIDTH), CONV_K),
        "ret_log_gamma": ret_log_gamma,
        "gdn_a_log": gdn_a_log,
        "gdn_dt_bias": gdn_dt_bias,
        "gdn_norm": gain(ks[13], (DEPTH, GDN_HEAD_DIM)),
        "w_out": dense(ks[14], (DEPTH, D_MIX, D_MODEL), D_MIX),
        "xattn_q": dense(ks[15], (DEPTH, D_MODEL, D_MODEL), D_MODEL),
        "xattn_k": dense(ks[16], (DEPTH, D_MODEL, D_MODEL), D_MODEL),
        "xattn_v": dense(ks[17], (DEPTH, D_MODEL, D_MODEL), D_MODEL),
        "xattn_o": dense(ks[18], (DEPTH, D_MODEL, D_MODEL), D_MODEL),
        "ffn2_gate": dense(ks[19], (DEPTH, D_MODEL, D_FF), D_MODEL),
        "ffn2_up": dense(ks[20], (DEPTH, D_MODEL, D_FF), D_MODEL),
        "ffn2_down": dense(ks[21], (DEPTH, D_FF, D_MODEL), D_FF),
    }

def first_block(x, mem, positions, norm_pre, norm_post, mem_norm, ffn1_gate, ffn1_up, ffn1_down,
              w_in, gdn_conv, ret_log_gamma, gdn_a_log, gdn_dt_bias, gdn_norm, w_out,
              xattn_q, xattn_k, xattn_v, xattn_o, ffn2_gate, ffn2_up, ffn2_down):
    cos, sin = rotary_tables(positions)
    for l in range(DEPTH):
        h = swiglu(rms_norm(x, norm_pre[l, 0]), ffn1_gate[l], ffn1_up[l], ffn1_down[l])
        x = x + 0.5 * rms_norm(h, norm_post[l, 0])
        h = parallel_head_groups(rms_norm(x, norm_pre[l, 1]), cos, sin, w_in[l], gdn_conv[l],
                                 ret_log_gamma[l], gdn_a_log[l], gdn_dt_bias[l], gdn_norm[l], w_out[l])
        x = x + rms_norm(h, norm_post[l, 1])
        h = memory_cross_attention(rms_norm(x, norm_pre[l, 2]), rms_norm(mem, mem_norm[l]),
                                   xattn_q[l], xattn_k[l], xattn_v[l], xattn_o[l])
        x = x + rms_norm(h, norm_post[l, 2])
        h = swiglu(rms_norm(x, norm_pre[l, 3]), ffn2_gate[l], ffn2_up[l], ffn2_down[l])
        x = x + 0.5 * rms_norm(h, norm_post[l, 3])
    return x


DEPTH_2 = 1

SSM_EXPAND = 2
SSM_D_INNER = SSM_EXPAND * D_MODEL
SSM_HEAD_DIM = 64
SSM_N_HEADS = SSM_D_INNER // SSM_HEAD_DIM
SSM_N_GROUPS = 4
SSM_D_STATE = 128
SSM_CONV = 4
SSM_CHUNK = 128
SSM_CONV_DIM = SSM_D_INNER + 2 * SSM_N_GROUPS * SSM_D_STATE

ATT_HEAD_DIM = 128
ATT_HEADS_PER_GROUP = 4
ATT_PATTERNS = ((128, 1), (512, 4), (2048, 16))
ATT_N_HEADS = ATT_HEADS_PER_GROUP * len(ATT_PATTERNS)
ATT_QKV_DIM = 3 * ATT_N_HEADS * ATT_HEAD_DIM
ATT_OUT_DIM = ATT_HEADS_PER_GROUP * ATT_HEAD_DIM
ATT_BLOCK = 128
ROPE_THETA = 10000.0

N_BRANCH = 2
D_FF_2 = -(-8 * D_MODEL // (3 * 256)) * 256
IN_PROJ_SIZES = (SSM_D_INNER, SSM_CONV_DIM, SSM_N_HEADS, ATT_QKV_DIM, N_BRANCH * D_MODEL)
IN_PROJ_DIM = sum(IN_PROJ_SIZES)
EPS = 1e-6


def rmsnorm(x, g):
    xf = x.astype(jnp.float32)
    y = xf * lax.rsqrt(jnp.mean(xf * xf, axis=-1, keepdims=True) + EPS)
    return (y * g.astype(jnp.float32)).astype(x.dtype)

def rope(t, pos):
    half = t.shape[-1] // 2
    inv = ROPE_THETA ** (-jnp.arange(half, dtype=jnp.float32) / half)
    ang = pos.astype(jnp.float32)[:, None] * inv[None, :]
    cos = jnp.cos(ang)[None, :, None, :]
    sin = jnp.sin(ang)[None, :, None, :]
    t1, t2 = t[..., :half], t[..., half:]
    return jnp.concatenate([t1 * cos - t2 * sin, t2 * cos + t1 * sin], axis=-1)

def segsum(a):
    T = a.shape[-1]
    xx = jnp.broadcast_to(a[..., :, None], a.shape + (T,))
    cs = jnp.cumsum(jnp.where(jnp.tril(jnp.ones((T, T), bool), -1), xx, 0.0), axis=-2)
    return jnp.where(jnp.tril(jnp.ones((T, T), bool)), cs, -jnp.inf)

def causal_depthwise_conv(u, w, b):
    K, C = w.shape
    out = lax.conv_general_dilated(u, w[:, None, :], window_strides=(1,), padding=[(K - 1, 0)],
                                   dimension_numbers=('NWC', 'WIO', 'NWC'), feature_group_count=C)
    return out + b

def ssd_chunked(xs, dt, A, Bm, Cm):
    b, S, H, P = xs.shape
    G, N = Bm.shape[-2:]
    J = H // G
    Q = SSM_CHUNK
    nc = S // Q
    xdt = (xs * dt[..., None]).reshape(b, nc, Q, G, J, P)
    a = (dt * A).reshape(b, nc, Q, G, J).transpose(0, 1, 3, 4, 2)
    a_cs = jnp.cumsum(a, axis=-1)
    Br = Bm.reshape(b, nc, Q, G, N)
    Cr = Cm.reshape(b, nc, Q, G, N)
    tri = jnp.tril(jnp.ones((Q, Q), bool))
    Lmat = jnp.exp(jnp.where(tri, a_cs[..., :, None] - a_cs[..., None, :], -jnp.inf))
    CB = jnp.einsum('bclgn,bcsgn->bcgls', Cr, Br)
    y_diag = jnp.einsum('bcgjls,bcsgjp->bclgjp', CB[:, :, :, None] * Lmat, xdt)
    decay_states = jnp.exp(a_cs[..., -1:] - a_cs)
    states = jnp.einsum('bclgn,bcgjl,bclgjp->bcgjpn', Br, decay_states, xdt)
    chunk_tot = jnp.pad(a_cs[..., -1].transpose(0, 2, 3, 1), ((0, 0), (0, 0), (0, 0), (1, 0)))
    decay_chunk = jnp.exp(segsum(chunk_tot))
    states = jnp.concatenate([jnp.zeros_like(states[:, :1]), states], axis=1)
    new_states = jnp.einsum('bgjzc,bcgjpn->bzgjpn', decay_chunk, states)
    prev_states = new_states[:, :-1]
    y_off = jnp.einsum('bclgn,bcgjpn,bcgjl->bclgjp', Cr, prev_states, jnp.exp(a_cs))
    return (y_diag + y_off).reshape(b, S, H, P)

def mamba2_branch(z, xBC, dt_raw, conv_w, conv_b, dt_bias, a_log, d_skip, ssm_norm):
    b, S, _ = z.shape
    xBC = jax.nn.silu(causal_depthwise_conv(xBC, conv_w, conv_b)).astype(jnp.float32)
    gn = SSM_N_GROUPS * SSM_D_STATE
    xs = xBC[..., :SSM_D_INNER].reshape(b, S, SSM_N_HEADS, SSM_HEAD_DIM)
    Bm = xBC[..., SSM_D_INNER:SSM_D_INNER + gn].reshape(b, S, SSM_N_GROUPS, SSM_D_STATE)
    Cm = xBC[..., SSM_D_INNER + gn:].reshape(b, S, SSM_N_GROUPS, SSM_D_STATE)
    dt = jax.nn.softplus(dt_raw.astype(jnp.float32) + dt_bias.astype(jnp.float32))
    A = -jnp.exp(a_log.astype(jnp.float32))
    y = ssd_chunked(xs, dt, A, Bm, Cm) + d_skip.astype(jnp.float32)[:, None] * xs
    y = y.reshape(b, S, SSM_D_INNER) * jax.nn.silu(z.astype(jnp.float32))
    yg = y.reshape(b, S, SSM_N_GROUPS, SSM_D_INNER // SSM_N_GROUPS)
    yg = yg * lax.rsqrt(jnp.mean(yg * yg, axis=-1, keepdims=True) + EPS)
    y = yg.reshape(b, S, SSM_D_INNER) * ssm_norm.astype(jnp.float32)
    return y.astype(z.dtype)

def dilated_window_group(q, k, v, window, dilation):
    b, S, h, d = q.shape
    r = dilation
    w_sub = window // r
    L = S // r
    nb = -(-L // ATT_BLOCK)
    Lp = nb * ATT_BLOCK

    def to_blocks(t):
        t = t.reshape(b, L, r, h, d).transpose(0, 2, 1, 3, 4)
        t = jnp.pad(t, ((0, 0), (0, 0), (0, Lp - L), (0, 0), (0, 0)))
        return t.reshape(b, r, nb, ATT_BLOCK, h, d)

    def with_prev(t):
        prev = jnp.pad(t[:, :, :-1], ((0, 0), (0, 0), (1, 0), (0, 0), (0, 0), (0, 0)))
        return jnp.concatenate([prev, t], axis=3)

    qb = to_blocks(q)
    kk = with_prev(to_blocks(k))
    vv = with_prev(to_blocks(v))
    s = jnp.einsum('brnqhd,brnkhd->brnhqk', qb, kk) * (d ** -0.5)
    qi = jnp.arange(ATT_BLOCK)[:, None]
    kj = jnp.arange(2 * ATT_BLOCK)[None, :]
    dist = qi + ATT_BLOCK - kj
    band = (dist >= 0) & (dist <= w_sub)
    has_prev = (jnp.arange(nb) > 0)[:, None, None] | (kj >= ATT_BLOCK)[None]
    mask = band[None] & has_prev
    s = jnp.where(mask[None, None, :, None], s, -jnp.inf)
    m = jnp.max(s, axis=-1, keepdims=True)
    p = jnp.exp(s - m)
    den = jnp.sum(p, axis=-1, keepdims=True)
    o = jnp.einsum('brnhqk,brnkhd->brnqhd', p / den, vv)
    lse = (m + jnp.log(den))[..., 0].transpose(0, 1, 2, 4, 3)
    o = o.reshape(b, r, Lp, h, d)[:, :, :L].transpose(0, 2, 1, 3, 4).reshape(b, S, h, d)
    lse = lse.reshape(b, r, Lp, h)[:, :, :L].transpose(0, 2, 1, 3).reshape(b, S, h)
    return o, lse

def dilated_attention_branch(q, k, v):
    outs, lses = [], []
    for gi, (window, dilation) in enumerate(ATT_PATTERNS):
        sl = slice(gi * ATT_HEADS_PER_GROUP, (gi + 1) * ATT_HEADS_PER_GROUP)
        o, lse = dilated_window_group(q[:, :, sl], k[:, :, sl], v[:, :, sl], window, dilation)
        outs.append(o)
        lses.append(lse)
    o = jnp.stack(outs, axis=0)
    wts = jax.nn.softmax(jnp.stack(lses, axis=0), axis=0)
    return jnp.sum(wts[..., None] * o, axis=0)

def second_inputs(seed: int = 0) -> dict:
    key = jax.random.key(seed)
    ks = jax.random.split(key, 20)
    f32 = jnp.float32

    def nrm(k, shape, scale):
        return jax.random.normal(k, shape, f32) * scale

    dt0 = jnp.exp(jax.random.uniform(ks[6], (DEPTH_2, SSM_N_HEADS), f32,
                                     minval=math.log(1e-3), maxval=math.log(1e-1)))
    return {
        "x": nrm(ks[0], (BATCH, SEQ, D_MODEL), 1.0),
        "norm_mix": 1.0 + nrm(ks[1], (DEPTH_2, D_MODEL), 0.05),
        "w_in": nrm(ks[2], (DEPTH_2, D_MODEL, IN_PROJ_DIM), D_MODEL ** -0.5),
        "b_gate": nrm(ks[3], (DEPTH_2, N_BRANCH * D_MODEL), 0.01),
        "conv_w": nrm(ks[4], (DEPTH_2, SSM_CONV, SSM_CONV_DIM), SSM_CONV ** -0.5),
        "conv_b": nrm(ks[5], (DEPTH_2, SSM_CONV_DIM), 0.01),
        "dt_bias": dt0 + jnp.log(-jnp.expm1(-dt0)),
        "a_log": jnp.log(jax.random.uniform(ks[7], (DEPTH_2, SSM_N_HEADS), f32, minval=1.0, maxval=16.0)),
        "d_skip": 1.0 + nrm(ks[8], (DEPTH_2, SSM_N_HEADS), 0.1),
        "ssm_norm": 1.0 + nrm(ks[9], (DEPTH_2, SSM_D_INNER), 0.05),
        "w_ssm_out": nrm(ks[10], (DEPTH_2, SSM_D_INNER, D_MODEL), SSM_D_INNER ** -0.5),
        "w_att_out": nrm(ks[11], (DEPTH_2, ATT_OUT_DIM, D_MODEL), ATT_OUT_DIM ** -0.5),
        "w_mix_out": nrm(ks[12], (DEPTH_2, D_MODEL, D_MODEL), D_MODEL ** -0.5),
        "norm_ffn": 1.0 + nrm(ks[13], (DEPTH_2, D_MODEL), 0.05),
        "w_ffn_gate": nrm(ks[14], (DEPTH_2, D_MODEL, D_FF_2), D_MODEL ** -0.5),
        "w_ffn_up": nrm(ks[15], (DEPTH_2, D_MODEL, D_FF_2), D_MODEL ** -0.5),
        "w_ffn_down": nrm(ks[16], (DEPTH_2, D_FF_2, D_MODEL), D_FF_2 ** -0.5),
        "norm_final": 1.0 + nrm(ks[17], (D_MODEL,), 0.05),
    }

def second_block(x, norm_mix, w_in, b_gate, conv_w, conv_b, dt_bias, a_log, d_skip, ssm_norm,
              w_ssm_out, w_att_out, w_mix_out, norm_ffn, w_ffn_gate, w_ffn_up, w_ffn_down, norm_final):
    b, S, _ = x.shape
    pos = jnp.arange(S)
    offs = [0]
    for sz in IN_PROJ_SIZES[:-1]:
        offs.append(offs[-1] + sz)
    for l in range(DEPTH_2):
        h = rmsnorm(x, norm_mix[l])
        proj = h @ w_in[l]
        z, xBC, dt_raw, qkv, gate_logits = jnp.split(proj, offs[1:], axis=-1)

        y_ssm = mamba2_branch(z, xBC, dt_raw, conv_w[l], conv_b[l], dt_bias[l], a_log[l],
                              d_skip[l], ssm_norm[l]) @ w_ssm_out[l]

        qkv = qkv.astype(jnp.float32).reshape(b, S, 3, ATT_N_HEADS, ATT_HEAD_DIM)
        q = rope(qkv[:, :, 0], pos)
        k = rope(qkv[:, :, 1], pos)
        v = qkv[:, :, 2]
        y_att = dilated_attention_branch(q, k, v).reshape(b, S, ATT_OUT_DIM).astype(x.dtype) @ w_att_out[l]

        gates = jax.nn.sigmoid((gate_logits + b_gate[l]).astype(jnp.float32))
        gates = gates.reshape(b, S, N_BRANCH, D_MODEL).astype(x.dtype)
        mixed = gates[:, :, 0] * y_ssm + gates[:, :, 1] * y_att
        x = x + mixed @ w_mix_out[l]

        h = rmsnorm(x, norm_ffn[l])
        x = x + (jax.nn.silu(h @ w_ffn_gate[l]) * (h @ w_ffn_up[l])) @ w_ffn_down[l]
    return rmsnorm(x, norm_final)


def setup_inputs(seed=0):
    out = dict(first_inputs(seed))
    for name, value in second_inputs(seed + 1).items():
        if name != "x":
            out[name + "_2"] = value
    return out


def reference(
    x, mem, positions, norm_pre, norm_post, mem_norm, ffn1_gate, ffn1_up, ffn1_down, w_in,
    gdn_conv, ret_log_gamma, gdn_a_log, gdn_dt_bias, gdn_norm, w_out, xattn_q, xattn_k, xattn_v,
    xattn_o, ffn2_gate, ffn2_up, ffn2_down, norm_mix_2, w_in_2, b_gate_2, conv_w_2, conv_b_2,
    dt_bias_2, a_log_2, d_skip_2, ssm_norm_2, w_ssm_out_2, w_att_out_2, w_mix_out_2, norm_ffn_2,
    w_ffn_gate_2, w_ffn_up_2, w_ffn_down_2, norm_final_2,
):
    x = first_block(
        x, mem, positions, norm_pre, norm_post, mem_norm, ffn1_gate, ffn1_up, ffn1_down, w_in,
        gdn_conv, ret_log_gamma, gdn_a_log, gdn_dt_bias, gdn_norm, w_out, xattn_q, xattn_k,
        xattn_v, xattn_o, ffn2_gate, ffn2_up, ffn2_down,
    )
    return second_block(
        x, norm_mix_2, w_in_2, b_gate_2, conv_w_2, conv_b_2, dt_bias_2, a_log_2, d_skip_2,
        ssm_norm_2, w_ssm_out_2, w_att_out_2, w_mix_out_2, norm_ffn_2, w_ffn_gate_2, w_ffn_up_2,
        w_ffn_down_2, norm_final_2,
    )


_drawn_inputs = setup_inputs


def setup_inputs(seed=0):
    import zlib

    import numpy as np

    out = dict(_drawn_inputs(seed))
    spreads = {}
    factors = {'gdn_norm': 3.676,
     'norm_mix_2': 3.123,
     'b_gate_2': 22.393,
     'conv_b_2': 8.0,
     'd_skip_2': 30.528,
     'ssm_norm_2': 5.119,
     'norm_ffn_2': 3.335}
    for name, (base, spread) in spreads.items():
        noise = np.random.default_rng([zlib.crc32(name.encode()), seed]).standard_normal(out[name].shape)
        drawn = base * np.exp(spread * noise) if base else spread * noise
        out[name] = __import__('jax').numpy.asarray(drawn.astype(out[name].dtype))
    for name, factor in factors.items():
        out[name] = (out[name] * factor).astype(out[name].dtype)
    return out
```

```python
from contextlib import ExitStack

import numpy as np
import concourse.bass as bass
from concourse import mybir

F32 = mybir.dt.float32
F32R = mybir.dt.float32r
I32 = mybir.dt.int32
AF = mybir.ActivationFunctionType
ALU = mybir.AluOpType
AX = mybir.AxisListType.X

P = 128
SEQ = 256
NT = SEQ // P
D = 1024
KT = D // P
FF = 2816
CH = FF // 256
DEPTH = 2
HEADS = 4
EPS = 1e-6
UNIT = 2048
RING = 3
LAYER_UNITS = 102
FFN_UNITS = 3 * CH
SECOND_UNITS = 93
N_UNITS = DEPTH * LAYER_UNITS + SECOND_UNITS
SSM_HEADS, SSM_GROUPS = 32, 4
ROWS_LAYER = 9
N_ROWS = DEPTH * ROWS_LAYER + 5
TWO_PI = 2.0 * np.pi

C_IDENT, C_ONES, C_UI, C_LI = 0, 128, 256, 384
C_REL = 512
C_INV = 1024
C_LEN = 1032


def shape_constants():
    c = np.zeros((P, C_LEN), np.float32)
    i = np.arange(P)
    c[:, C_IDENT:C_IDENT + P] = np.eye(P)
    c[:, C_ONES:C_ONES + P] = 1.0
    c[:, C_UI:C_UI + P] = i[None, :] >= i[:, None]
    c[:, C_LI:C_LI + P] = i[None, :] <= i[:, None]
    n = np.arange(SEQ)
    for t in range(NT):
        c[:, C_REL + t * SEQ:C_REL + (t + 1) * SEQ] = n[None, :] - (i[:, None] + t * P)
    inv = (10000.0 ** (-np.arange(0, P, 2, dtype=np.float32) / np.float32(P))).astype(np.float32)
    c[:, C_INV] = np.concatenate([inv, inv])
    c[:, C_INV + 1] = np.where(i < 64, -1.0, 1.0)
    return c


def level_masks():
    i = np.arange(P)
    m = np.zeros((P, 7, P), np.float32)
    for l in range(7):
        s = 1 << l
        m[:, l] = (i[:, None] // (2 * s) == i[None, :] // (2 * s)) & (i[:, None] // s != i[None, :] // s)
    return m.reshape(P, 7 * P)


def attention_masks():
    m = np.zeros((P, 3, NT, SEQ), np.float32)
    k = np.arange(SEQ)
    for g, (window, dil) in enumerate(((128, 1), (512, 4), (2048, 16))):
        for t in range(NT):
            dist = (np.arange(P) + t * P)[:, None] - k[None, :]
            ok = (dist >= 0) & (dist % dil == 0) & (dist <= window)
            m[:, g, t] = np.where(ok, 0.0, -1e30)
    return m.reshape(P, 3 * NT * SEQ)


def rope_tables():
    half = np.arange(64, dtype=np.float32)
    inv = (np.float32(10000.0) ** (-half / np.float32(64))).astype(np.float32)
    ang = (np.arange(SEQ, dtype=np.float32)[None, :] * inv[:, None]).astype(np.float64)
    cos, sin = np.cos(ang), np.sin(ang)
    return np.concatenate([np.concatenate([cos, cos]), np.concatenate([-sin, sin])], axis=1).astype(np.float32)


class Prog:

    def __init__(self, eng):
        self.e, self.n = eng, {}
        self.i, self.per = None, {}

    def count(self, name, k=1):
        self.n[name] = self.n.get(name, 0) + k
        return self.value(name, self.n[name])

    def skip(self, name, k=1):
        self.n[name] = self.n.get(name, 0) + k

    def value(self, name, value):
        return value if self.i is None else self.i * self.per[name] + value

    def loop(self, iters, per):
        return _Loop(self, iters, per)


class _Loop:
    def __init__(self, prog, iters, per):
        self.p, self.iters, self.per_iter = prog, iters, per

    def __enter__(self):
        self.before = dict(self.p.n)
        self.cm = self.p.e.Fori(0, self.iters)
        self.p.per = self.per_iter
        self.p.i = self.cm.__enter__()
        return self.p.i

    def __exit__(self, *exc):
        self.p.i = None
        r = self.cm.__exit__(*exc)
        if exc[0] is None:
            for name, n in self.p.n.items():
                d = n - self.before.get(name, 0)
                if d:
                    assert d == self.per_iter[name], (name, d)
                    self.p.n[name] = self.before.get(name, 0) + self.iters * d
        return r


def build(nc, a, out):
    ctx = ExitStack()
    with ctx:
        def sb(name, shape, dt=F32):
            return ctx.enter_context(nc.sbuf_tensor(name, shape, dt))

        class Sems(dict):

            def __missing__(self, name):
                self[name] = ctx.enter_context(nc.semaphore(name))
                return self[name]
        sems = Sems()

        raw = [sb(f"raw{i}", [P, UNIT]) for i in range(RING)]
        whi = [sb(f"whi{i}", [P, UNIT], F32R) for i in range(RING)]
        wlo = [sb(f"wlo{i}", [P, UNIT], F32R) for i in range(RING)]
        x = sb("x", [P, NT, D])
        uT = [sb("uT_hi", [P, KT, SEQ], F32R), sb("uT_lo", [P, KT, SEQ], F32R)]
        mT = [sb("memT_hi", [P, KT, SEQ], F32R), sb("memT_lo", [P, KT, SEQ], F32R)]
        hT = [sb("hT_hi", [P, 4, SEQ], F32R), sb("hT_lo", [P, 4, SEQ], F32R)]
        rows = sb("rows", [P, 3, D])
        cst = sb("cst", [P, C_LEN])
        lvl = sb("lvl", [P, 7 * P], mybir.dt.bfloat16)
        msk4 = sb("msk4", [P, 4, P], mybir.dt.bfloat16)
        small = sb("small", [P, 488])
        st = sb("st", [P, 64])
        A = 15616
        arena = sb("arena", [P, A])
        bank = [ctx.enter_context(nc.psum_tensor(f"bank{i}", [P, 512], F32)) for i in range(8)]

        ident = cst[:, C_IDENT:C_IDENT + P]
        ones = cst[:, C_ONES:C_ONES + P]
        UI = cst[:, C_UI:C_UI + P]
        LI = cst[:, C_LI:C_LI + P]

        def view(off, *dims):
            n = int(np.prod(dims))
            v = arena[:, off:off + n]
            if len(dims) == 2:
                return v.rearrange("p (a b) -> p a b", a=dims[0])
            if len(dims) == 3:
                return v.rearrange("p (a b c) -> p a b c", a=dims[0], b=dims[1])
            return v

        sg = [view(0 + 512 * i, 512) for i in range(2)]
        hb = [view(1024 + 512 * i, 512) for i in range(2)]
        posi = view(13360, 256).bitcast(I32)
        turns, angle = view(13616, 256), view(13872, 256)
        lvl_f32 = view(14128, 7 * P)
        ub = view(6192, NT, D)
        tmpn = view(8240, NT, D)
        junk = view(10288, D)
        memx = view(11312, NT, D)
        cin = view(0, 12, 260)
        sq = view(0, 8, 256)
        cout = view(3120, 12, 256)
        rqT = view(6192, 4, 256)
        rkT = view(7216, 4, 256)
        rv = view(8240, NT, 512)
        osb = view(9264, NT, D)
        dret = [view(11312 + 512 * i, 2, 256) for i in range(2)]
        stb = [view(12336 + 512 * i, 2, 256) for i in range(2)]
        kx = view(11312, KT, 256)
        ktok = view(13360, NT, 512)
        vtok = view(14384, NT, 512)
        sw = [view(13360 + 512 * i, 2, 256) for i in range(2)]
        rt = [view(14384 + 512 * i, 2, 256) for i in range(2)]
        G = []
        for off in (0, 6192):
            G.append([view(off + 512 * i, 4, P) for i in range(6)])
        ab = [hT[i][:, 0, 0:P] for i in range(2)]
        abT = view(2560, SEQ)
        qx = view(0, KT, 256)
        vx = [view(3120 + 256 * tile, NT, 256) for tile in (8, 10, 0, 4)]
        px = [view(6192 + 512 * i, 2, 256) for i in range(2)]
        pxT = [view(7216 + 512 * i, 2, 256) for i in range(2)]
        S_LG, S_AL, S_DT, S_GN, S_CV, S_AB = 0, 8, 16, 24, 152, 212
        S_LEN = 340
        cosT = sb("cosT", [P, SEQ])
        sinT = sb("sinT", [P, SEQ])
        gat = sb("gat", [P, 2, 48])

        cin2 = view(0, 6, 260)
        cout2 = view(1560, 6, 256)
        zg = view(3096, NT, 512)
        xs = view(4120, NT, 512)
        xdt = view(5144, NT, 512)
        xdec = view(6168, 512)
        btok = view(6680, P)
        Eb = [view(6808 + 512 * i, 4, P) for i in range(2)]
        cbm = view(7832, 256)
        Ssb = view(8088, 512)
        ytmp = view(8600, NT, 512)
        junk2 = view(9624, 512)
        gs = view(11264, 2, 192)
        amask = view(12032, 3, 2, 256)
        ysb = view(13568, NT, D)
        qa = view(0, 3, 2, 256)
        ka = view(1536, 3, 2, 256)
        va = view(3072, 3, 2, 256)
        Pb = [view(4608 + 1536 * i, 3, 2, 256) for i in range(2)]
        PTb = view(7680, 3, 2, 256)
        sw2 = [view(9216 + 512 * i, 2, 256) for i in range(2)]
        rt2 = [view(10240 + 512 * i, 2, 256) for i in range(2)]
        gates = view(0, 16, 256)
        mixed = view(4096, KT, 256)
        mixt = view(6144, 2, 256)
        Z_DT, Z_AL, Z_DS, Z_CW, Z_CB, Z_BG, Z_WD = 0, 32, 64, 96, 192, 216, 232
        Z_LEN = 488
        b2 = DEPTH * LAYER_UNITS
        att0 = b2 + 5 * SSM_GROUPS
        qk_bank = ((2, 3, 4, 5, 2, 3), (2, 1, 4, 5, 2, 1))
        gate_bank = (2, 1, 4, 5)
        conv_bank, z_bank = (2, 3, 6), (2, 3)
        wdt = [hT[i][:, 0, :] for i in range(2)]
        dtT = view(10400, SEQ)

        def blocks(v, l, odd):
            w = v.rearrange("p c (n q s) -> p (c n) q s", q=2, s=1 << l) if len(v.shape) == 3 else \
                v.rearrange("p (n q s) -> p n q s", q=2, s=1 << l)
            return w[:, :, odd, :]

        def compact(b, dr, l):
            return b[:, dr * P:(dr + 1) * P].rearrange("p (n s) -> p n s", s=1 << l)

        block = ctx.enter_context(nc.Block())

        @block.sync
        def _(sp):
            p = Prog(sp)
            sp.dma_start(cst[:, 0:P], a["cst"][:, 0:P]).then_inc(sems["ident_in"], 16)
            sp.dma_start(x[:], a["x"]).then_inc(sems["x_in"], 16)
            for s in range(RING):
                sp.dma_start(raw[s][:], a["w"][s]).then_inc(sems[f"raw_landed{s}"], 16)
            sp.dma_start(cst[:, P:], a["cst"][:, P:]).then_inc(sems["cst_in"], 16)
            sp.dma_start(posi, a["pos"].to_broadcast((P, SEQ))).then_inc(sems["pos_in"], 16)
            sp.dma_start(lvl_f32, a["lvl"]).then_inc(sems["lvl_in"], 16)
            with p.loop(N_UNITS // RING - 1, {"w_lo": RING}) as i:
                for s in range(RING):
                    sp.wait_ge(sems["w_lo"], p.count("w_lo"))
                    sp.dma_start(raw[s][:], a["w"][i * RING + (RING + s)]).then_inc(sems[f"raw_landed{s}"], 16)
            sp.wait_ge(sems["out_ready"], 1)
            sp.dma_start(out[0].rearrange("(t p) d -> p t d", p=P), x[:]).then_inc(sems["stored"], 16)
            sp.wait_ge(sems["stored"], 16)

        @block.gpsimd
        def _(pool):
            p = Prog(pool)
            with p.loop(N_UNITS // RING, {"w_hi": RING}):
                for s in range(RING):
                    pool.wait_ge(sems["w_hi"], p.count("w_hi"))
                    pool.tensor_tensor(wlo[s][:], raw[s][:], whi[s][:].bitcast(F32), ALU.subtract)\
                        .then_inc(sems["w_lo"], 1)

        @block.scalar
        def _(act):
            p = Prog(act)
            state = {"split": 0, "row": 0}

            def fn(o, i, f, **k):
                return act.activation(o, i, f, **k)

            def split(k=1):
                for _ in range(k):
                    n = state["split"]
                    if n >= N_UNITS:
                        return
                    s = n % RING
                    act.wait_ge(sems[f"raw_landed{s}"], p.count(f"raw_landed{s}", 16))
                    if n >= RING:
                        act.wait_ge(sems["unit_done"], p.value("unit_done", n - RING + 1))
                    fn(whi[s][:], raw[s][:], AF.Copy).then_inc(sems["w_hi"], 1)
                    state["split"] += 1

            def split_to(u):
                split(max(0, min(u + RING, N_UNITS) - state["split"]))

            def row():
                r = state["row"]
                if r < N_ROWS:
                    act.dma_start(rows[:, r % 3, :], a["rows"][r:r + 1, :].to_broadcast((P, D)))\
                        .then_inc(sems[f"row_landed{r % 3}"], 16)
                state["row"] += 1

            def root_table():
                fn(st[:, 62:63], st[:, 60:61], AF.Sqrt)

            def root(o, i, n, eps=None):
                act.drain()
                return fn(o, i, AF.Sqrt, scale=1.0 / n, bias=st[:, 60:61] if eps is None else eps)

            def prenorm(src, ready):
                for t in range(NT):
                    if ready:
                        act.wait_ge(sems[ready], p.count(ready))
                    fn(junk[:, :], src[:, t, :], AF.Square, accum_out=st[:, t:t + 1])
                    root(st[:, t:t + 1], st[:, t:t + 1], D).then_inc(sems["rms"], 1)

            def hi_parts(dst, banks):
                for n, b in enumerate(banks):
                    act.wait_ge(sems[f"act_bank{b}"], p.count(f"act_bank{b}"))
                    fn(dst[0][:, 2 * n:2 * n + 2, :], bank[b][:, :].rearrange("p (a b) -> p a b", a=2), AF.Copy)\
                        .then_inc(sems["hi_part"], 1)

            def postnorm(u_last, half):
                for t in range(NT):
                    if t == 0:
                        act.wait_ge(sems["first_rows"], p.count("first_rows"))
                    else:
                        act.wait_ge(sems["unit_done"], p.value("unit_done", u_last + 1))
                    for h in range(2):
                        fn(junk[:, h * 512:(h + 1) * 512], bank[2 * t + h][:, :], AF.Square,
                           accum_out=st[:, 4 + 2 * t + h:5 + 2 * t + h]).then_inc(sems["squared"], 1)
                    act.drain()
                    fn(st[:, 2 + t:3 + t], st[:, 4 + 2 * t:5 + 2 * t], AF.Identity, bias=st[:, 5 + 2 * t:6 + 2 * t])
                    root(st[:, 2 + t:3 + t], st[:, 2 + t:3 + t], D * half * half,
                         st[:, 60:61] if half == 1.0 else st[:, 61:62]).then_inc(sems["rms"], 1)

            def ffn(u0, between=None, late=None):
                def chunk(c, g, last=False):
                    q = c % 2
                    act.wait_ge(sems["unit_done"], p.value("unit_done", g + 1))
                    fn(sg[q], bank[4 + 2 * q][:, :], AF.Silu).then_inc(sems["silu_gate"], 1)
                    split()
                    act.wait_ge(sems["ff_product"], p.count("ff_product"))
                    fn(hT[0][:, 2 * q:2 * q + 2, :], hb[q].rearrange("p (a b) -> p a b", a=2), AF.Copy)\
                        .then_inc(sems["h_hi"], 1)
                    if last:
                        root_table()
                    split(2)
                split_to(u0)
                act.wait_ge(sems["unit_done"], p.value("unit_done", u0 + 1))
                fn(sg[0], bank[4][:, :], AF.Silu).then_inc(sems["silu_gate"], 1)
                split()
                act.wait_ge(sems["ff_product"], p.count("ff_product"))
                fn(hT[0][:, 0:2, :], hb[0].rearrange("p (a b) -> p a b", a=2), AF.Copy).then_inc(sems["h_hi"], 1)
                split()
                if between:
                    between()
                chunk(1, u0 + 2)
                chunk(2, u0 + 5)
                per = {"unit_done": 6, "raw_landed0": 32, "raw_landed1": 32, "raw_landed2": 32,
                       "ff_product": 2}
                s0 = state["split"]
                with p.loop((CH - 5) // 2, per):
                    chunk(3, u0 + 8)
                    chunk(4, u0 + 11)
                state["split"] = s0 + 6 * ((CH - 5) // 2)
                if late:
                    late()
                chunk(CH - 2, u0 + 3 * (CH - 2) - 1)
                chunk(CH - 1, u0 + 3 * (CH - 1) - 1, last=True)
                return u0 + 32

            row()
            act.wait_ge(sems["eps_set"], p.count("eps_set"))
            root_table()
            act.wait_ge(sems["x_in"], 16)

            def rotary_tables():
                act.wait_ge(sems["angle"], p.count("angle"))
                fn(cosT[:, :], angle, AF.Sin, scale=0.5)
                fn(sinT[:, :], angle, AF.Sin)
                act.drain()
                fn(cosT[:, :], cosT[:, :], AF.Square)
                act.drain()
                fn(cosT[:, :], cosT[:, :], AF.Copy, scale=-2.0, bias=1.0).then_inc(sems["trig"], 1)

            def memory_norm():
                act.wait_ge(sems["mem_in"], p.count("mem_in", 16))
                prenorm(memx, None)
                hi_parts(mT, (0, 1, 2, 3))
                row()

            for L in range(DEPTH):
                base = L * LAYER_UNITS
                prenorm(x, "x_ready" if L else None)
                if L == 0:
                    split(2)
                else:
                    split_to(base)
                hi_parts(uT, (4, 5, 6, 7))
                row()
                act.dma_start(memx, a["mem"]).then_inc(sems["mem_in"], 16)
                row()
                if L == 0:
                    row()
                    act.dma_start(small[:, 0:S_LEN], a["small"][0]).then_inc(sems["small_in"], 16)
                last = ffn(base, memory_norm, None if L else rotary_tables)
                split_to(last)
                postnorm(last, 0.5)
                prenorm(x, "x_ready")
                hi_parts(uT, (4, 5, 6, 7))
                row()
                row()
                m0 = base + FFN_UNITS
                split_to(m0)
                act.wait_ge(sems["conv_pad"], p.count("conv_pad"))
                for j in range(6):
                    act.wait_ge(sems["unit_done"], p.value("unit_done", m0 + j + 1))
                    fn(cin[:, 2 * j:2 * j + 2, 2:258], bank[j][:, :].rearrange("p (a b) -> p a b", a=2), AF.Copy)\
                        .then_inc(sems["conv_in"], 1)
                    split_to(m0 + j + 1)

                def conv_out(g):
                    act.wait_ge(sems["conv"], p.count("conv"))
                    r = fn(cout[:, 4 * g:4 * g + 4, :], cout[:, 4 * g:4 * g + 4, :], AF.Silu)
                    if g < 2:
                        act.drain()
                        fn(sq[:, 4 * g:4 * g + 4, :], cout[:, 4 * g:4 * g + 4, :], AF.Square).then_inc(sems["squares"], 1)
                    else:
                        r.then_inc(sems["v_ready"], 1)

                def tok_out(j, b):
                    u = m0 + 10 + j
                    act.wait_ge(sems["unit_done"], p.value("unit_done", u + 1))
                    bv = bank[b][:, :].rearrange("p (a b) -> p a b", a=2)
                    if j < 2:
                        fn(rv[:, :, j * 256:(j + 1) * 256], bv, AF.Copy).then_inc(sems["tok_out"], 1)
                    else:
                        fn(osb[:, :, (j - 2) * 256:(j - 1) * 256], bv, AF.Silu).then_inc(sems["tok_out"], 1)
                    split_to(u + 1)

                def ret_decay(h):
                    act.wait_ge(sems["ret_arg"], p.count("ret_arg"))
                    fn(dret[h % 2], dret[h % 2], AF.Exp).then_inc(sems["ret_decay"], 1)

                conv_out(0)
                for j in range(4):
                    u = m0 + 6 + j
                    b = (6, 7, 0, 1)[j]
                    act.wait_ge(sems["unit_done"], p.value("unit_done", u + 1))
                    bv = bank[b][:, :].rearrange("p (a b) -> p a b", a=2)
                    if j >= 2:
                        act.wait_ge(sems["rotated"], p.count("rotated"))
                    fn(sw[j % 2][0:64], bv[64:128], AF.Copy)
                    fn(sw[j % 2][64:128], bv[0:64], AF.Copy).then_inc(sems["swapped"], 1)
                    split_to(u + 1)
                    if j < 2:
                        conv_out(j + 1)
                    if j == 1:
                        act.wait_ge(sems["small_in"], p.count("small_in", 16))
                        fn(ab[0], small[:, S_AB:S_AB + P], AF.Copy).then_inc(sems["ab_hi"], 1)
                p.skip("rotated", 2)
                for j in range(4):
                    b = 2 + j
                    act.wait_ge(sems[f"act_bank{b}"], p.count(f"act_bank{b}"))
                    fn(sq[:, 2 * j:2 * j + 2, :], bank[b][:, :].rearrange("p (a b) -> p a b", a=2), AF.Ln, bias=st[:, 60:61])\
                        .then_inc(sems[f"act_read{b}"], 1)
                act.drain()
                for j in range(4):
                    o = sq[:, 2 * j:2 * j + 2, :]
                    fn(o, o, AF.Exp, scale=-0.5).then_inc(sems["l2_scale"], 1)
                fn(st[:, 32:40], small[:, S_AL:S_AL + 8], AF.Exp)
                ret_decay(0)
                ret_decay(1)
                tok_out(0, 6)
                tok_out(1, 7)
                tok_out(2, 1)
                act.wait_ge(sems["gate_in"], p.count("gate_in"))
                fn(gat[:, :, 8:16], gat[:, :, 8:16], AF.Exp, scale=-1.0)
                fn(gat[:, :, 16:24], gat[:, :, 16:24], AF.Exp, scale=-1.0)
                ret_decay(2)
                ret_decay(3)
                act.drain()
                fn(gat[:, :, 8:16], gat[:, :, 8:16], AF.Ln, bias=1.0).then_inc(sems["softplus"], 1)
                tok_out(3, 4)
                tok_out(4, 7)
                act.wait_ge(sems["cs_cols"], p.count("cs_cols"))
                fn(gat[:, :, 32:40], gat[:, :, 24:32], AF.Exp)
                fn(gat[:, :, 40:48], gat[:, :, 40:48], AF.Exp).then_inc(sems["col_decay"], 1)
                tok_out(5, 1)
                act.wait_ge(sems["ret_sq"], p.count("ret_sq", 2))
                root(st[:, 12:20], st[:, 12:20], P).then_inc(sems["ret_rms"], 1)

                def memory_out(n):
                    u = m0 + 16 + n
                    act.wait_ge(sems["unit_done"], p.value("unit_done", u + 1))
                    fn(kx[:, 2 * n:2 * n + 2, :] if n < 4 else vx[n - 4],
                       bank[(3, 7)[n % 2]][:, :].rearrange("p (a b) -> p a b", a=2), AF.Copy)\
                        .then_inc(sems[f"act_read{(3, 7)[n % 2]}"], 1)
                    split_to(u + 1)
                memory_out(0)
                for j in range(4):
                    b = (0, 4, 5, 6)[j]
                    act.wait_ge(sems[f"act_bank{b}"], p.count(f"act_bank{b}"))
                    fn((ktok if j < 2 else vtok)[:, j % 2, :], bank[b][:, :], AF.Copy).then_inc(sems[f"act_read{b}"], 1)
                for pair in range(2):
                    for s in range(2):
                        act.wait_ge(sems["decay_arg"], p.count("decay_arg"))
                        fn(G[s][0], G[s][0], AF.Exp).then_inc(sems["decay"], 1)
                    memory_out(1 + 4 * pair)
                    for s in range(2):
                        act.wait_ge(sems[f"act_bank{4 * s + 2}"], p.count(f"act_bank{4 * s + 2}"))
                        fn(G[s][4], bank[4 * s + 2][:, :].rearrange("p (a b) -> p a b", a=4), AF.Copy)\
                            .then_inc(sems["t_first"], 1)
                    for l in range(1, 7):
                        for s in range(2):
                            act.wait_ge(sems[f"act_bank{4 * s}"], p.count(f"act_bank{4 * s}"))
                            fn(G[s][0], bank[4 * s][:, :].rearrange("p (a b) -> p a b", a=4), AF.Copy)\
                                .then_inc(sems[f"act_read{4 * s}"], 1)
                    memory_out(2 + 4 * pair)
                    for s in range(2):
                        act.wait_ge(sems[f"act_bank{4 * s + 1}"], p.count(f"act_bank{4 * s + 1}"))
                        fn(G[s][2][:, 0:2, :], bank[4 * s + 1][:, 0:256].rearrange("p (a b) -> p a b", a=2), AF.Copy)\
                            .then_inc(sems[f"act_read{4 * s + 1}"], 1)
                    if pair == 0:
                        memory_out(3)
                        memory_out(4)
                root_table()
                act.wait_ge(sems["gdn_sq"], p.count("gdn_sq"))
                root(st[:, 20:28], st[:, 20:28], P).then_inc(sems["gdn_rms"], 1)
                memory_out(7)
                hi_parts(uT, (4, 5, 6, 7))
                last = m0 + 27
                split_to(last - 1)
                root_table()
                split_to(last)
                postnorm(last, 1.0)
                prenorm(x, "x_ready")
                hi_parts(uT, (4, 5, 6, 7))
                row()
                row()

                def query_out(h):
                    u = m0 + 28 + h
                    act.wait_ge(sems["unit_done"], p.value("unit_done", u + 1))
                    fn(qx[:, 2 * h:2 * h + 2, :], bank[h][:, :].rearrange("p (a b) -> p a b", a=2), AF.Copy)\
                        .then_inc(sems[f"act_read{h}"], 1)
                    split_to(u + 1)

                def exponentials_x(h):
                    act.wait_ge(sems["xmax"], p.count("xmax"))
                    for t in range(NT):
                        r = fn(px[h % 2][:, t, :], bank[4 + h][:, t * 256:(t + 1) * 256], AF.Exp, scale=1.0 / 16,
                               bias=st[:, 2 * h + t + 12:2 * h + t + 13], accum_out=st[:, 2 * h + t + 20:2 * h + t + 21])
                    r.then_inc(sems["xexp"], 1)

                def probs_out_x(h):
                    act.wait_ge(sems[f"act_bank{h}"], p.count(f"act_bank{h}"))
                    fn(pxT[h % 2], bank[h][:, :].rearrange("p (a b) -> p a b", a=2), AF.Copy)\
                        .then_inc(sems[f"act_read{h}"], 1)

                def head_hi_x(h):
                    act.wait_ge(sems[f"act_bank{4 + h}"], p.count(f"act_bank{4 + h}"))
                    fn(uT[0][:, 2 * h:2 * h + 2, :], bank[4 + h][:, :].rearrange("p (a b) -> p a b", a=2), AF.Copy)\
                        .then_inc(sems["hi_part"], 1)
                split_to(m0 + 28)
                query_out(0)
                query_out(1)
                exponentials_x(0)
                query_out(2)
                exponentials_x(1)
                probs_out_x(0)
                query_out(3)
                exponentials_x(2)
                head_hi_x(0)
                probs_out_x(1)
                exponentials_x(3)
                head_hi_x(1)
                for h in (2, 3):
                    probs_out_x(h)
                    head_hi_x(h)
                last = m0 + 35
                split_to(last - 1)
                root_table()
                split_to(last)
                postnorm(last, 1.0)
                prenorm(x, "x_ready")
                split_to(base + 69)
                hi_parts(uT, (4, 5, 6, 7))
                row()
                row()
                last = ffn(base + 69)
                if L == 0:
                    act.dma_start(small[:, 0:S_LEN], a["small"][1]).then_inc(sems["small_in"], 16)
                split_to(last)
                postnorm(last, 0.5)

            def half2(b):
                return bank[b][:, :].rearrange("p (a b) -> p a b", a=2)

            act.dma_start(small[:, 0:Z_LEN], a["small2"]).then_inc(sems["small_in"], 16)
            act.dma_start(cosT[:, :], a["rope"][:, 0:SEQ]).then_inc(sems["rope_in"], 16)
            act.dma_start(sinT[:, :], a["rope"][:, SEQ:2 * SEQ]).then_inc(sems["rope_in"], 16)
            prenorm(x, "x_ready")
            split_to(b2)
            hi_parts(uT, (4, 5, 6, 7))
            row()
            row()
            act.dma_start(view(12032, 1536), a["amask"]).then_inc(sems["amask_in"], 16)
            act.wait_ge(sems["small_in"], p.count("small_in", 16))
            fn(wdt[0], small[:, Z_WD:Z_WD + 256], AF.Copy).then_inc(sems["wdt_hi"], 1)
            act.wait_ge(sems["conv_pad"], p.count("conv_pad"))

            def conv_in(g, j):
                u = b2 + 5 * g + j
                act.wait_ge(sems["unit_done"], p.value("unit_done", u + 1))
                fn(cin2[:, 2 * j:2 * j + 2, 3:259], half2(conv_bank[j]), AF.Copy).then_inc(sems["conv_in"], 1)
                split_to(u + 1)

            def conv_silu(part):
                act.wait_ge(sems["conv"], p.count("conv"))
                v = cout2[:, 4:6, :] if part else cout2[:, 0:4, :]
                fn(v, v, AF.Silu).then_inc(sems["conv_silu"], 1)

            conv_in(0, 0)
            conv_in(0, 1)
            conv_in(0, 2)
            fn(small[:, Z_AL:Z_AL + 32], small[:, Z_AL:Z_AL + 32], AF.Exp)
            act.wait_ge(sems["gate_in"], p.count("gate_in"))
            fn(gs[:, :, 160:192], gs[:, :, 160:192], AF.Exp, scale=-1.0)
            act.drain()
            fn(gs[:, :, 160:192], gs[:, :, 160:192], AF.Ln, bias=1.0).then_inc(sems["softplus"], 1)
            for g in range(SSM_GROUPS):
                for j in range(2):
                    u = b2 + 5 * g + 3 + j
                    act.wait_ge(sems["unit_done"], p.value("unit_done", u + 1))
                    fn(zg[:, :, j * 256:(j + 1) * 256], half2(z_bank[j]), AF.Silu).then_inc(sems["tok_out"], 1)
                    split_to(u + 1)
                    if j == 0:
                        if g == 0:
                            conv_silu(0)
                        conv_silu(1)
                if g == 2:
                    hi_parts(mT, (0, 1, 4, 5))
                if g == 0:
                    act.wait_ge(sems["cs_cols"], p.count("cs_cols"))
                    fn(gs[:, :, 96:128], gs[:, :, 64:96], AF.Exp)
                    fn(gs[:, :, 128:160], gs[:, :, 128:160], AF.Exp).then_inc(sems["col_decay"], 1)
                for c in range(2):
                    b = (1, 7)[c]
                    act.wait_ge(sems[f"act_bank{b}"], p.count(f"act_bank{b}"))
                    fn(xs[:, c, :], bank[b][:, :], AF.Copy).then_inc(sems["xs_out"], 1)
                if g < SSM_GROUPS - 1:
                    conv_in(g + 1, 0)
                else:
                    act.wait_ge(sems["unit_done"], p.value("unit_done", att0 + 1))
                    split_to(att0 + 1)
                act.wait_ge(sems["act_bank0"], p.count("act_bank0"))
                fn(Ssb, bank[0][:, :], AF.Copy).then_inc(sems["act_read0"], 1)
                for hp in range(4):
                    if hp == 2 and g < SSM_GROUPS - 1:
                        conv_in(g + 1, 1)
                    elif hp == 2:
                        act.wait_ge(sems["unit_done"], p.value("unit_done", att0 + 2))
                        split_to(att0 + 2)
                    act.wait_ge(sems["ssm_arg"], p.count("ssm_arg"))
                    fn(Eb[hp % 2], Eb[hp % 2], AF.Exp).then_inc(sems["ssm_decay"], 1)
                if g < SSM_GROUPS - 1:
                    conv_silu(0)
                    conv_in(g + 1, 2)
                for t in range(NT):
                    act.wait_ge(sems["y_raw"], p.count("y_raw"))
                    fn(junk2, ysb[:, t, (g % 2) * 512:(g % 2 + 1) * 512], AF.Square, accum_out=st[:, 10 + t:11 + t])
                    root(st[:, 10 + t:11 + t], st[:, 10 + t:11 + t], 512).then_inc(sems["y_rms"], 1)

            def swap(pr, j):
                u = att0 + 9 * pr + j
                act.wait_ge(sems["unit_done"], p.value("unit_done", u + 1))
                bv = half2(qk_bank[pr][j])
                if pr or j >= 2:
                    act.wait_ge(sems["rotated"], p.count("rotated"))
                fn(sw2[j % 2][0:64], bv[64:128], AF.Copy)
                fn(sw2[j % 2][64:128], bv[0:64], AF.Copy).then_inc(sems["swapped"], 1)
                split_to(u + 1)

            def value_out(pr, g):
                u = att0 + 9 * pr + 6 + g
                act.wait_ge(sems["unit_done"], p.value("unit_done", u + 1))
                fn(va[:, g], half2((6, 7, 6)[g]), AF.Copy).then_inc(sems["tok_out"], 1)
                split_to(u + 1)

            def gate_out(j):
                u = att0 + 18 + j
                act.wait_ge(sems["unit_done"], p.value("unit_done", u + 1))
                for q in range(2):
                    i = 2 * j + q
                    r = fn(gates[:, i, :], bank[gate_bank[j % 4]][:, q * SEQ:(q + 1) * SEQ], AF.Sigmoid,
                           bias=small[:, Z_BG + i:Z_BG + i + 1])
                r.then_inc(sems["gates_out"], 1)
                split_to(u + 1)

            def exponentials(hh):
                for g in range(3):
                    act.wait_ge(sems["att_max"], p.count("att_max"))
                    for t in range(NT):
                        c = 2 * g + t
                        fn(Pb[hh][:, g, t, :], Pb[hh][:, g, t, :], AF.Exp, bias=gat[:, hh, c:c + 1],
                           accum_out=gat[:, hh, c + 6:c + 7])

            def probs_out():
                for g in range(3):
                    b = (6, 7, 0)[g]
                    act.wait_ge(sems[f"act_bank{b}"], p.count(f"act_bank{b}"))
                    fn(PTb[:, g], half2(b), AF.Copy).then_inc(sems["probs_T"], 1)

            def head_out(pr, hh):
                act.wait_ge(sems["act_bank3"], p.count("act_bank3"))
                fn(hT[0][:, 2 * pr + hh, :], bank[3][:, 0:SEQ], AF.Copy).then_inc(sems["hi_part"], 1)

            split_to(att0)
            for j in range(6):
                swap(0, j)
            for pr in range(2):
                value_out(pr, 0)
                exponentials(0)
                value_out(pr, 1)
                exponentials(1)
                value_out(pr, 2)
                act.drain()
                fn(gat[:, :, 12:18], gat[:, :, 6:12], AF.Ln).then_inc(sems["att_ln"], 1)
                act.wait_ge(sems["lse_rel"], p.count("lse_rel"))
                fn(gat[:, :, 24:30], gat[:, :, 24:30], AF.Exp).then_inc(sems["att_weight"], 1)
                for n in range(4):
                    if n == 2:
                        probs_out()
                    if n == 3:
                        head_out(pr, 0)
                        probs_out()
                    if pr == 0:
                        swap(1, n)
                    else:
                        gate_out(n)
                head_out(pr, 1)
                if pr == 0:
                    swap(1, 4)
                    swap(1, 5)
                else:
                    for n in range(4, 8):
                        gate_out(n)
            p.skip("rotated", 2)
            split_to(b2 + 46)
            hi_parts(uT, (0, 1, 2, 3))
            split_to(b2 + 55)
            for n in range(4):
                act.wait_ge(sems["mixed"], p.count("mixed"))
                fn(uT[0][:, 2 * n:2 * n + 2, :], mixed[:, 2 * n:2 * n + 2, :], AF.Copy).then_inc(sems["hi_part"], 1)
            split_to(b2 + 58)
            root_table()
            split_to(b2 + 59)
            prenorm(x, "x_ready")
            split_to(b2 + 60)
            hi_parts(uT, (4, 5, 6, 7))
            row()
            last = ffn(b2 + 60)
            for t in range(NT):
                act.wait_ge(sems["x_ready"], p.count("x_ready"))
                fn(junk[:, :], x[:, t, :], AF.Square, accum_out=st[:, t:t + 1])
                root(st[:, t:t + 1], st[:, t:t + 1], D).then_inc(sems["rms"], 1)

        @block.vector
        def _(dve):
            p = Prog(dve)
            state = {"row": 0}
            tt, ts, stt = dve.tensor_tensor, dve.tensor_scalar, dve.scalar_tensor_tensor

            def use_row():
                r = state["row"]
                state["row"] += 1
                dve.wait_ge(sems[f"row_landed{r % 3}"], p.count(f"row_landed{r % 3}", 16))
                return rows[:, r % 3, :]

            def prenorm(src):
                w = use_row()
                for t in range(NT):
                    dve.wait_ge(sems["rms"], p.count("rms"))
                    dve.reciprocal(st[:, t:t + 1], st[:, t:t + 1])
                    dve.drain()
                    stt(ub[:, t, :], src[:, t, :], st[:, t:t + 1], w, ALU.mult, ALU.mult).then_inc(sems["u_ready"], 1)

            def lo_parts(dst, banks):
                for n, b in enumerate(banks):
                    dve.wait_ge(sems["hi_part"], p.count("hi_part"))
                    k = slice(2 * n, 2 * n + 2)
                    tt(dst[1][:, k, :], bank[b][:, :].rearrange("p (a b) -> p a b", a=2), dst[0][:, k, :].bitcast(F32),
                       ALU.subtract).then_inc(sems[f"dve_read{b}"], 1)

            def postnorm():
                w = use_row()
                for t in range(NT):
                    for h in range(2):
                        c = slice(h * 512, (h + 1) * 512)
                        dve.wait_ge(sems["squared"], p.count("squared"))
                        tt(tmpn[:, t, c], bank[2 * t + h][:, :], w[:, c], ALU.mult).then_inc(sems[f"dve_read{2 * t + h}"], 1)
                    dve.wait_ge(sems["rms"], p.count("rms"))
                    dve.reciprocal(st[:, 2 + t:3 + t], st[:, 2 + t:3 + t])
                    dve.drain()
                    stt(x[:, t, :], tmpn[:, t, :], st[:, 2 + t:3 + t], x[:, t, :], ALU.mult, ALU.add).then_inc(sems["x_ready"], 1)
                p.skip("first_rows")

            def ffn(u0, between=None):
                def chunk(c, g):
                    q = c % 2
                    dve.wait_ge(sems["silu_gate"], p.count("silu_gate"))
                    dve.wait_ge(sems["unit_done"], p.value("unit_done", g + 2))
                    tt(hb[q], sg[q], bank[5 + 2 * q][:, :], ALU.mult).then_inc(sems["ff_product"], 1)
                    dve.drain()
                    dve.wait_ge(sems["h_hi"], p.count("h_hi"))
                    tt(hT[1][:, 2 * q:2 * q + 2, :], hb[q].rearrange("p (a b) -> p a b", a=2),
                       hT[0][:, 2 * q:2 * q + 2, :].bitcast(F32), ALU.subtract).then_inc(sems["h_lo"], 1)
                chunk(0, u0)
                if between:
                    between()
                chunk(1, u0 + 2)
                chunk(2, u0 + 5)
                with p.loop((CH - 3) // 2, {"unit_done": 6, "silu_gate": 2, "h_hi": 2}):
                    chunk(3, u0 + 8)
                    chunk(4, u0 + 11)
                return u0 + 32

            dve.memset(st[:, 60:61], EPS)
            dve.memset(st[:, 61:62], 4 * EPS)
            dve.memset(st[:, 0:60], 0.0).then_inc(sems["eps_set"], 1)
            dve.wait_ge(sems["x_in"], p.count("x_in", 16))

            def rotary_angles():
                dve.wait_ge(sems["cst_in"], p.count("cst_in", 16))
                dve.wait_ge(sems["pos_in"], p.count("pos_in", 16))
                dve.tensor_copy(turns, posi)
                dve.drain()
                ts(angle, turns, cst[:, C_INV:C_INV + 1], None, ALU.mult)
                dve.drain()
                ts(turns, angle, float(1.0 / TWO_PI), 12582912.0, ALU.mult, ALU.add)
                dve.drain()
                ts(turns, turns, 12582912.0, None, ALU.subtract)
                dve.drain()
                c1 = 6.28125
                c2 = float(np.float32(np.round((TWO_PI - c1) * 2 ** 20) / 2 ** 20))
                c3 = float(np.float32(TWO_PI - c1 - c2))
                for c in (c1, c2, c3):
                    stt(angle, turns, -c, angle, ALU.mult, ALU.add)
                    dve.drain()
                ts(angle, angle, float(np.float32(3.1415925)), float(np.float32(-3.1415925)), ALU.min, ALU.max)\
                    .then_inc(sems["angle"], 1)
                for i, m in enumerate((UI, UI, LI, LI)):
                    dve.tensor_copy(msk4[:, i, :], m)
                dve.wait_ge(sems["lvl_in"], p.count("lvl_in", 16))
                dve.tensor_copy(lvl[:, :], lvl_f32)

            def memory_norm():
                prenorm(memx)
                lo_parts(mT, (0, 1, 2, 3))

            def memory_norm_and_tables():
                memory_norm()
                rotary_angles()

            for L in range(DEPTH):
                base = L * LAYER_UNITS
                prenorm(x)
                lo_parts(uT, (4, 5, 6, 7))
                ffn(base, memory_norm if L else memory_norm_and_tables)
                if L == 0:
                    dve.wait_ge(sems["trig"], p.count("trig"))
                    ts(sinT[:, :], sinT[:, :], cst[:, C_INV + 1:C_INV + 2], None, ALU.mult)
                postnorm()
                dve.memset(cin[:, :, 0:2], 0.0)
                dve.memset(cin[:, :, 258:260], 0.0).then_inc(sems["conv_pad"], 1)
                prenorm(x)
                lo_parts(uT, (4, 5, 6, 7))
                m0 = base + FFN_UNITS
                dve.wait_ge(sems["small_in"], p.count("small_in", 16))
                cv = small[:, S_CV:S_CV + 60].rearrange("p (a b) -> p a b", a=12)
                def rotate():
                    for j in range(4):
                        b = (6, 7, 0, 1)[j]
                        bv = bank[b][:, :].rearrange("p (a b) -> p a b", a=2)
                        dst = (rqT, rkT)[j // 2][:, 2 * (j % 2):2 * (j % 2) + 2, :]
                        dve.wait_ge(sems["swapped"], p.count("swapped"))
                        tt(rt[j % 2], bv, cosT[:, None, :].to_broadcast((P, 2, SEQ)), ALU.mult)\
                            .then_inc(sems[f"dve_read{b}"], 1)
                        tt(sw[j % 2], sw[j % 2], sinT[:, None, :].to_broadcast((P, 2, SEQ)), ALU.mult)
                        dve.drain()
                        tt(dst, rt[j % 2], sw[j % 2], ALU.add).then_inc(sems["rotated"], 1)
                for g in range(3):
                    for j in range(2 * g, 2 * g + 2):
                        dve.wait_ge(sems["conv_in"], p.count("conv_in"))
                    for k in range(5):
                        for i in range(4 * g, 4 * g + 4):
                            src = cin[:, i, k:k + 256]
                            if k == 0:
                                r = ts(cout[:, i, :], src, cv[:, i, 0:1], None, ALU.mult)
                            else:
                                r = stt(cout[:, i, :], src, cv[:, i, k:k + 1], cout[:, i, :], ALU.mult, ALU.add)
                        if k < 4:
                            dve.drain()
                    r.then_inc(sems["conv"], 1)
                dve.wait_ge(sems["ab_hi"], p.count("ab_hi"))
                tt(ab[1], small[:, S_AB:S_AB + P], ab[0].bitcast(F32), ALU.subtract).then_inc(sems["ab_lo"], 1)
                rotate()
                rel = cst[:, C_REL:C_REL + 512].rearrange("p (a b) -> p a b", a=2)

                def ret_arg(h):
                    ts(dret[h % 2], rel, 0.0, small[:, S_LG + h:S_LG + h + 1], ALU.max, ALU.mult)
                    ts(sw[h % 2], rel, 0.0, small[:, S_LG + 4 + h:S_LG + 5 + h], ALU.min, ALU.mult)
                    dve.drain()
                    tt(dret[h % 2], dret[h % 2], sw[h % 2], ALU.subtract).then_inc(sems["ret_arg"], 1)

                def ret_scores(h):
                    b = 2 + h % 2
                    dve.wait_ge(sems["ret_decay"], p.count("ret_decay"))
                    dve.wait_ge(sems[f"dve_bank{b}"], p.count(f"dve_bank{b}"))
                    stt(stb[h % 2], bank[b][:, :].rearrange("p (a b) -> p a b", a=2), float(P) ** -0.5, dret[h % 2],
                        ALU.mult, ALU.mult).then_inc(sems[f"dve_read{b}"], 1)
                dve.drain()
                ret_arg(0)
                ret_arg(1)
                for j in range(4):
                    dve.wait_ge(sems["l2_scale"], p.count("l2_scale"))
                    k = slice(2 * j, 2 * j + 2)
                    stt(cout[:, k, :], cout[:, k, :], float(P) ** -0.5 if j < 2 else 1.0, sq[:, k, :], ALU.mult, ALU.mult)\
                        .then_inc(sems["qk_unit"], 1)
                dve.wait_ge(sems["dve_bank0"], p.count("dve_bank0"))
                dve.tensor_copy(abT[0:16, :], bank[0][0:16, 0:SEQ]).then_inc(sems["dve_read0"], 1)
                dve.wait_ge(sems["dve_bank0"], p.count("dve_bank0"))
                abk = bank[0][:, 0:32].rearrange("p (t c) -> p t c", t=2)
                dtb = small[:, S_DT:S_DT + 8][:, None, :].to_broadcast((P, 2, 8))
                tt(gat[:, :, 0:8], abk[:, :, 0:8], dtb, ALU.add)
                dve.tensor_copy(gat[:, :, 16:24], abk[:, :, 8:16]).then_inc(sems["dve_read0"], 1)
                dve.drain()
                stt(gat[:, :, 8:16], gat[:, :, 0:8], -1.0, gat[:, :, 0:8], ALU.mult, ALU.max)
                ts(gat[:, :, 0:8], gat[:, :, 0:8], 0.0, None, ALU.max).then_inc(sems["gate_in"], 1)
                ret_scores(0)
                ret_scores(1)
                dve.drain()
                ret_arg(2)
                ret_arg(3)
                dve.wait_ge(sems["softplus"], p.count("softplus"))
                tt(gat[:, :, 0:8], gat[:, :, 0:8], gat[:, :, 8:16], ALU.add)
                ts(gat[:, :, 16:24], gat[:, :, 16:24], 1.0, None, ALU.add)
                dve.drain()
                stt(gat[:, :, 0:8], gat[:, :, 0:8], -1.0, st[:, 32:40][:, None, :].to_broadcast((P, 2, 8)),
                    ALU.mult, ALU.mult).then_inc(sems["g_ready"], 1)
                dve.reciprocal(gat[:, :, 16:24], gat[:, :, 16:24])
                for h in (2, 3):
                    dve.wait_ge(sems["st_used"], p.count("st_used"))
                    ret_scores(h)
                dve.wait_ge(sems["dve_bank0"], p.count("dve_bank0"))
                bc = bank[0][:, 0:32].rearrange("p (t c) -> p t c", t=2)
                dve.tensor_copy(gat[:, :, 24:32], bc[:, :, 0:8])
                dve.drain()
                tt(gat[:, :, 40:48], bc[:, :, 8:16], gat[:, :, 24:32], ALU.subtract).then_inc(sems["dve_read0"], 1)
                dve.drain().then_inc(sems["cs_cols"], 1)
                for t in range(NT):
                    b = 5 + t
                    ot = rt[t].rearrange("p a b -> p (a b)").rearrange("p (h d) -> p h d", h=4)
                    sqt = sw[t].rearrange("p a b -> p (a b)").rearrange("p (h d) -> p h d", h=4)
                    dve.wait_ge(sems[f"dve_bank{b}"], p.count(f"dve_bank{b}"))
                    bv = bank[b][:, :].rearrange("p (h d) -> p h d", h=4)
                    dve.tensor_reduce(st[:, 12 + 4 * t:16 + 4 * t], bv, AX, ALU.add)
                    dve.drain()
                    ts(st[:, 12 + 4 * t:16 + 4 * t], st[:, 12 + 4 * t:16 + 4 * t], 1.0 / P, None, ALU.mult)
                    dve.drain()
                    tt(ot, bv, st[:, 12 + 4 * t:16 + 4 * t][:, :, None].to_broadcast((P, 4, P)), ALU.subtract)\
                        .then_inc(sems[f"dve_read{b}"], 1)
                    dve.drain()
                    tt(sqt, ot, ot, ALU.mult)
                    dve.drain()
                    dve.tensor_reduce(st[:, 12 + 4 * t:16 + 4 * t], sqt, AX, ALU.add).then_inc(sems["ret_sq"], 1)
                for t in range(NT):
                    ot = rt[t].rearrange("p a b -> p (a b)").rearrange("p (h d) -> p h d", h=4)
                    if t == 0:
                        dve.wait_ge(sems["tok_out"], p.count("tok_out", 6))
                        dve.wait_ge(sems["ret_rms"], p.count("ret_rms"))
                        dve.reciprocal(st[:, 12:20], st[:, 12:20])
                        dve.drain()
                    tt(ot, ot, st[:, 12 + 4 * t:16 + 4 * t][:, :, None].to_broadcast((P, 4, P)), ALU.mult)
                    dve.drain()
                    tt(osb[:, t, 0:512], osb[:, t, 0:512], rt[t].rearrange("p a b -> p (a b)"), ALU.mult)\
                        .then_inc(sems["ret_done"], 1)
                m4 = msk4[:, :, :]
                for pair in range(2):
                    for s in range(2):
                        h = 2 * pair + s
                        DT, LT, LM, PT, T, TT = G[s]
                        dve.wait_ge(sems[f"dve_bank{4 * s}"], p.count(f"dve_bank{4 * s}"))
                        for i in range(4):
                            c, dr = i % 2, i // 2
                            r = ts(DT[:, i, :], bank[4 * s][:, i * P:(i + 1) * P], gat[:, c, 24 + 4 * dr + h:25 + 4 * dr + h],
                                   0.0, ALU.subtract, ALU.min)
                        r.then_inc(sems[f"dve_read{4 * s}"], 1)
                        dve.drain().then_inc(sems["decay_arg"], 1)
                    for s in range(2):
                        h = 2 * pair + s
                        DT, LT, LM, PT, T, TT = G[s]
                        dve.wait_ge(sems["decay"], p.count("decay"))
                        tt(DT, DT, m4, ALU.mult)
                        dve.wait_ge(sems[f"dve_bank{4 * s + 1}"], p.count(f"dve_bank{4 * s + 1}"))
                        dve.drain()
                        bG = bank[4 * s + 1]
                        for i in range(4):
                            c, dr = i % 2, i // 2
                            stt(LT[:, i, :], bG[:, c * P:(c + 1) * P], gat[:, c, 16 + 4 * dr + h:17 + 4 * dr + h],
                                DT[:, i, :], ALU.mult, ALU.mult)
                        for dr in range(2):
                            r = tt(PT[:, 2 * dr:2 * dr + 2, :], bG[:, 256:512].rearrange("p (a b) -> p a b", a=2),
                                   DT[:, 2 * dr:2 * dr + 2, :], ALU.mult)
                        r.then_inc(sems[f"dve_read{4 * s + 1}"], 1)
                        dve.drain()
                        tt(T, LT, lvl[:, 0:P][:, None, :].to_broadcast((P, 4, P)), ALU.mult)
                        dve.drain()
                        tt(TT, ident[:, None, :].to_broadcast((P, 4, P)), T, ALU.subtract).then_inc(sems["tt_first"], 1)

                    def level_part(s, l):
                        tt(G[s][2], G[s][1], lvl[:, l * P:(l + 1) * P][:, None, :].to_broadcast((P, 4, P)), ALU.mult)\
                            .then_inc(sems["level"], 1)
                    level_part(0, 1)
                    level_part(1, 1)
                    for l in range(1, 7):
                        for s in range(2):
                            DT, LT, LM, PT, T, TT = G[s]
                            if l < 6:
                                dve.wait_ge(sems["level_used"], p.count("level_used"))
                                level_part(s, l + 1)
                            if l == 1:
                                dve.wait_ge(sems["t_first"], p.count("t_first"))
                            dve.wait_ge(sems[f"dve_bank{4 * s + 1}"], p.count(f"dve_bank{4 * s + 1}"))
                            for dr in range(2):
                                o = blocks(TT[:, 2 * dr:2 * dr + 2, :], l, 1 - dr)
                                r = tt(o, o, compact(bank[4 * s + 1], dr, l), ALU.subtract)
                            r.then_inc(sems[f"dve_read{4 * s + 1}"], 1)
                            if l < 6:
                                for dr in range(2):
                                    o = blocks(T[:, 2 * dr:2 * dr + 2, :], l, dr)
                                    r = tt(o, o, compact(bank[4 * s + 2], dr, l), ALU.subtract)
                                r.then_inc(sems[f"dve_read{4 * s + 2}"], 1)
                    for s in range(2):
                        h = 2 * pair + s
                        DT, LT, LM, PT, T, TT = G[s]
                        hc = slice(h * P, (h + 1) * P)
                        if pair == 0 and s == 0:
                            dve.wait_ge(sems["col_decay"], p.count("col_decay"))
                        dve.wait_ge(sems[f"dve_bank{4 * s}"], p.count(f"dve_bank{4 * s}"))
                        for dr in range(2):
                            cA = dr
                            ts(LT[:, dr, :], ktok[:, cA, hc], gat[:, cA, 40 + 4 * dr + h:41 + 4 * dr + h], None, ALU.mult)
                            r = ts(T[:, 2 * dr + cA, :], bank[4 * s][:, dr * P:(dr + 1) * P],
                                   gat[:, cA, 16 + 4 * dr + h:17 + 4 * dr + h], None, ALU.mult)
                        r.then_inc(sems[f"dve_read{4 * s}"], 1)
                    for s in range(2):
                        h = 2 * pair + s
                        DT, LT, LM, PT, T, TT = G[s]
                        hc = slice(h * P, (h + 1) * P)
                        dve.wait_ge(sems[f"dve_bank{4 * s + 2}"], p.count(f"dve_bank{4 * s + 2}"))
                        bk = bank[4 * s + 2]
                        for dr in range(2):
                            cB = 1 - dr
                            eg = gat[:, cB, 32 + 4 * dr + h:33 + 4 * dr + h]
                            ts(LT[:, 2 + dr, :], bk[:, dr * P:(dr + 1) * P], eg, -1.0, ALU.mult, ALU.mult)
                            r = ts(DT[:, dr, :], bk[:, 256 + dr * P:256 + (dr + 1) * P], eg, None, ALU.mult)
                        r.then_inc(sems[f"dve_read{4 * s + 2}"], 1)
                        dve.drain()
                        for dr in range(2):
                            r = tt(LT[:, 2 + dr, :], LT[:, 2 + dr, :], vtok[:, 1 - dr, hc], ALU.add)
                        r.then_inc(sems["rest"], 1)
                    for s in range(2):
                        h = 2 * pair + s
                        DT, LT, LM, PT, T, TT = G[s]
                        dve.wait_ge(sems[f"dve_bank{4 * s + 1}"], p.count(f"dve_bank{4 * s + 1}"))
                        for dr in range(2):
                            cB = 1 - dr
                            r = ts(T[:, 2 * dr + cB, :], bank[4 * s + 1][:, dr * P:(dr + 1) * P],
                                   gat[:, cB, 16 + 4 * dr + h:17 + 4 * dr + h], None, ALU.mult)
                        r.then_inc(sems[f"dve_read{4 * s + 1}"], 1)
                    for s in range(2):
                        h = 2 * pair + s
                        DT, LT, LM, PT, T, TT = G[s]
                        hc = slice(h * P, (h + 1) * P)
                        dve.wait_ge(sems[f"dve_bank{4 * s}"], p.count(f"dve_bank{4 * s}"))
                        for c in range(2):
                            r = tt(vtok[:, c, hc], bank[4 * s][:, c * P:(c + 1) * P], DT[:, 1 - c, :], ALU.add)
                        r.then_inc(sems[f"dve_read{4 * s}"], 1)
                v8 = vtok.rearrange("p t (h d) -> p (t h) d", h=4)
                k8 = ktok.rearrange("p t (h d) -> p (t h) d", h=4)
                dve.drain()
                tt(k8, v8, v8, ALU.mult)
                dve.drain()
                dve.tensor_reduce(st[:, 20:28], k8, AX, ALU.add).then_inc(sems["gdn_sq"], 1)
                gn = small[:, S_GN:S_GN + P][:, None, :].to_broadcast((P, 8, P))
                tt(v8, v8, gn, ALU.mult)
                dve.wait_ge(sems["gdn_rms"], p.count("gdn_rms"))
                dve.reciprocal(st[:, 20:28], st[:, 20:28])
                dve.drain()
                tt(v8, v8, st[:, 20:28][:, :, None].to_broadcast((P, 8, P)), ALU.mult)
                dve.drain()
                for t in range(NT):
                    tt(osb[:, t, 512:1024], osb[:, t, 512:1024], vtok[:, t, :], ALU.mult).then_inc(sems["mix_ready"], 1)
                lo_parts(uT, (4, 5, 6, 7))
                postnorm()
                prenorm(x)
                lo_parts(uT, (4, 5, 6, 7))

                def softmax_x(h):
                    b = 4 + h
                    dve.wait_ge(sems[f"dve_bank{b}"], p.count(f"dve_bank{b}"))
                    nm = st[:, 12 + 2 * h:14 + 2 * h]
                    den = st[:, 20 + 2 * h:22 + 2 * h]
                    dve.tensor_reduce(nm, bank[b][:, :].rearrange("p (a b) -> p a b", a=2), AX, ALU.max)
                    dve.drain()
                    ts(nm, nm, -1.0 / 16, None, ALU.mult).then_inc(sems["xmax"], 1)
                    dve.wait_ge(sems["xexp"], p.count("xexp"))
                    dve.reciprocal(den, den)
                    dve.drain()
                    for t in range(NT):
                        r = ts(px[h % 2][:, t, :], px[h % 2][:, t, :], den[:, t:t + 1], None, ALU.mult)
                    r.then_inc(sems["xprob"], 1)

                def head_lo_x(h):
                    dve.wait_ge(sems["hi_part"], p.count("hi_part"))
                    tt(uT[1][:, 2 * h:2 * h + 2, :], bank[4 + h][:, :].rearrange("p (a b) -> p a b", a=2),
                       uT[0][:, 2 * h:2 * h + 2, :].bitcast(F32), ALU.subtract).then_inc(sems[f"dve_read{4 + h}"], 1)
                for h in range(3):
                    softmax_x(h)
                head_lo_x(0)
                softmax_x(3)
                for h in range(1, HEADS):
                    head_lo_x(h)
                postnorm()
                prenorm(x)
                lo_parts(uT, (4, 5, 6, 7))
                ffn(base + 69)
                postnorm()

            def half2(b):
                return bank[b][:, :].rearrange("p (a b) -> p a b", a=2)

            def heads(v):
                return v.rearrange("p (h d) -> p h d", h=8)

            prenorm(x)
            lo_parts(uT, (4, 5, 6, 7))
            dve.memset(cin2[:, :, 0:3], 0.0).then_inc(sems["conv_pad"], 1)
            dve.wait_ge(sems["small_in"], p.count("small_in", 16))
            dve.wait_ge(sems["rope_in"], p.count("rope_in", 32))
            dve.wait_ge(sems["wdt_hi"], p.count("wdt_hi"))
            tt(wdt[1], small[:, Z_WD:Z_WD + 256], wdt[0].bitcast(F32), ALU.subtract).then_inc(sems["wdt_lo"], 1)
            dve.wait_ge(sems["dve_bank0"], p.count("dve_bank0"))
            dve.tensor_copy(dtT[0:32, :], bank[0][0:32, 0:SEQ]).then_inc(sems["dve_read0"], 1)
            dve.wait_ge(sems["dve_bank0"], p.count("dve_bank0"))
            dtr = bank[0][:, 0:64].rearrange("p (t c) -> p t c", t=2)
            tt(gs[:, :, 0:32], dtr, small[:, Z_DT:Z_DT + 32][:, None, :].to_broadcast((P, 2, 32)), ALU.add)\
                .then_inc(sems["dve_read0"], 1)
            dve.drain()
            stt(gs[:, :, 160:192], gs[:, :, 0:32], -1.0, gs[:, :, 0:32], ALU.mult, ALU.max)
            ts(gs[:, :, 0:32], gs[:, :, 0:32], 0.0, None, ALU.max).then_inc(sems["gate_in"], 1)
            cw = small[:, Z_CW:Z_CW + 96].rearrange("p (a b) -> p a b", a=24)

            def convolve(g, part):
                dve.wait_ge(sems["conv_in"], p.count("conv_in", 1 if part else 2))
                for k in range(4):
                    for i in ((4, 5) if part else (0, 1, 2, 3)):
                        ch = 6 * g + i
                        src = cin2[:, i, k:k + 256]
                        if k == 0:
                            r = ts(cout2[:, i, :], src, cw[:, ch, 0:1], small[:, Z_CB + ch:Z_CB + ch + 1], ALU.mult, ALU.add)
                        else:
                            r = stt(cout2[:, i, :], src, cw[:, ch, k:k + 1], cout2[:, i, :], ALU.mult, ALU.add)
                    if k < 3:
                        dve.drain()
                r.then_inc(sems["conv"], 1)
            for g in range(SSM_GROUPS):
                if g == 0:
                    convolve(0, 0)
                    convolve(0, 1)
                    dve.wait_ge(sems["softplus"], p.count("softplus"))
                    dve.drain()
                    tt(gs[:, :, 0:32], gs[:, :, 0:32], gs[:, :, 160:192], ALU.add)
                    dve.drain()
                    stt(gs[:, :, 32:64], gs[:, :, 0:32], -1.0, small[:, Z_AL:Z_AL + 32][:, None, :].to_broadcast((P, 2, 32)),
                        ALU.mult, ALU.mult).then_inc(sems["g_ready"], 1)
                    dve.wait_ge(sems["dve_bank1"], p.count("dve_bank1"))
                    bc = bank[1][:, 0:128].rearrange("p (t c) -> p t c", t=2)
                    dve.tensor_copy(gs[:, :, 64:96], bc[:, :, 0:32])
                    dve.drain()
                    tt(gs[:, :, 128:160], bc[:, :, 32:64], gs[:, :, 64:96], ALU.subtract).then_inc(sems["dve_read1"], 1)
                    dve.drain().then_inc(sems["cs_cols"], 1)
                if g == 2:
                    lo_parts(mT, (0, 1, 4, 5))
                dve.wait_ge(sems["dve_bank0"], p.count("dve_bank0"))
                tt(cbm.rearrange("p (a b) -> p a b", a=2), bank[0][:, 0:256].rearrange("p (a b) -> p a b", a=2),
                   UI[:, None, :].to_broadcast((P, 2, P)), ALU.mult)
                dve.tensor_copy(btok, bank[0][:, 256:384]).then_inc(sems["dve_read0"], 1)
                if g == 0:
                    dve.wait_ge(sems["col_decay"], p.count("col_decay"))
                dve.wait_ge(sems["xs_out"], p.count("xs_out", 2))
                hs = slice(8 * g, 8 * g + 8)

                def bc8(off, c):
                    return gs[:, c, off + 8 * g:off + 8 * g + 8][:, :, None].to_broadcast((P, 8, 64))
                for c in range(2):
                    tt(heads(xdt[:, c, :]), heads(xs[:, c, :]), bc8(0, c), ALU.mult)
                dve.drain()
                tt(heads(xdec), heads(xdt[:, 0, :]), bc8(128, 0), ALU.mult).then_inc(sems["x_dt"], 1)
                for hp in range(4):
                    b = 4 + hp % 2
                    E = Eb[hp % 2]
                    dve.wait_ge(sems[f"dve_bank{b}"], p.count(f"dve_bank{b}"))
                    if hp >= 2:
                        dve.wait_ge(sems["m_used"], p.count("m_used"))
                    for i in range(4):
                        c, h = i % 2, 8 * g + 2 * hp + i // 2
                        r = ts(E[:, i, :], bank[b][:, i * P:(i + 1) * P], gs[:, c, 64 + h:65 + h], 0.0, ALU.subtract, ALU.min)
                    r.then_inc(sems[f"dve_read{b}"], 1)
                    dve.drain().then_inc(sems["ssm_arg"], 1)
                    dve.wait_ge(sems["ssm_decay"], p.count("ssm_decay"))
                    E2 = E.rearrange("p a b -> p (a b)").rearrange("p (a b) -> p a b", a=2)
                    tt(E2, E2, cbm[:, None, :].to_broadcast((P, 2, 256)), ALU.mult).then_inc(sems["m_ready"], 1)
                p.skip("m_used", 1)
                ds8 = small[:, Z_DS + 8 * g:Z_DS + 8 * g + 8][:, :, None].to_broadcast((P, 8, 64))
                for c in range(2):
                    tt(heads(ytmp[:, c, :]), heads(xs[:, c, :]), ds8, ALU.mult)
                dve.wait_ge(sems["dve_bank0"], p.count("dve_bank0"))
                tt(heads(xdec), heads(bank[0][:, :]), bc8(96, 1), ALU.mult).then_inc(sems["dve_read0"], 1)
                dve.drain()
                tt(ytmp[:, 1, :], ytmp[:, 1, :], xdec, ALU.add)
                dve.drain()
                if g < SSM_GROUPS - 1:
                    convolve(g + 1, 0)
                yc = slice((g % 2) * 512, (g % 2 + 1) * 512)
                dve.wait_ge(sems["tok_out"], p.count("tok_out", 2))
                for c in range(2):
                    b = (1, 7)[c]
                    dve.wait_ge(sems[f"dve_bank{b}"], p.count(f"dve_bank{b}"))
                    tt(ytmp[:, c, :], bank[b][:, :], ytmp[:, c, :], ALU.add).then_inc(sems[f"dve_read{b}"], 1)
                dve.drain()
                for c in range(2):
                    tt(ysb[:, c, yc], ytmp[:, c, :], zg[:, c, :], ALU.mult).then_inc(sems["y_raw"], 1)
                if g < SSM_GROUPS - 1:
                    convolve(g + 1, 1)
                if g % 2 == 0:
                    w = use_row()
                for c in range(2):
                    dve.wait_ge(sems["y_rms"], p.count("y_rms"))
                    dve.reciprocal(st[:, 10 + c:11 + c], st[:, 10 + c:11 + c])
                    dve.drain()
                    stt(ysb[:, c, yc], ysb[:, c, yc], st[:, 10 + c:11 + c], w[:, yc], ALU.mult, ALU.mult)\
                        .then_inc(sems["y_ready"], 1)
            dve.wait_ge(sems["amask_in"], p.count("amask_in", 16))

            def rotate(pr, j):
                g, kind = j // 2, j % 2
                dve.wait_ge(sems["swapped"], p.count("swapped"))
                tt(rt2[j % 2], half2(qk_bank[pr][j]), cosT[:, None, :].to_broadcast((P, 2, SEQ)), ALU.mult)\
                    .then_inc(sems[f"dve_read{qk_bank[pr][j]}"], 1)
                tt(sw2[j % 2], sw2[j % 2], sinT[:, None, :].to_broadcast((P, 2, SEQ)), ALU.mult)
                dve.drain()
                tt((qa, ka)[kind][:, g], rt2[j % 2], sw2[j % 2], ALU.add).then_inc(sems["rotated"], 1)

            def head_lo(pr, hh):
                dve.wait_ge(sems["hi_part"], p.count("hi_part"))
                tt(hT[1][:, 2 * pr + hh, :], bank[3][:, 0:SEQ], hT[0][:, 2 * pr + hh, :].bitcast(F32), ALU.subtract)\
                    .then_inc(sems["dve_read3"], 1)

            def by_pattern(v):
                return v.rearrange("p h (g t) -> p h g t", g=3)

            for j in range(6):
                rotate(0, j)
            for pr in range(2):
                for hh in range(2):
                    for g in range(3):
                        b = 3 * hh + g
                        dve.wait_ge(sems[f"dve_bank{b}"], p.count(f"dve_bank{b}"))
                        stt(Pb[hh][:, g], half2(b), float(P) ** -0.5, amask[:, g], ALU.mult, ALU.add)\
                            .then_inc(sems[f"dve_read{b}"], 1)
                        dve.drain()
                        nm = gat[:, hh, 2 * g:2 * g + 2]
                        dve.tensor_reduce(nm, Pb[hh][:, g], AX, ALU.max)
                        dve.drain()
                        ts(nm, nm, -1.0, None, ALU.mult).then_inc(sems["att_max"], 1)
                dve.wait_ge(sems["att_ln"], p.count("att_ln"))
                tt(gat[:, :, 18:24], gat[:, :, 12:18], gat[:, :, 0:6], ALU.subtract)
                dve.drain()
                M = gat[:, :, 30:32]
                tt(M, gat[:, :, 18:20], gat[:, :, 20:22], ALU.max)
                dve.drain()
                tt(M, M, gat[:, :, 22:24], ALU.max)
                dve.drain()
                tt(by_pattern(gat[:, :, 24:30]), by_pattern(gat[:, :, 18:24]), M[:, :, None, :].to_broadcast((P, 2, 3, 2)),
                   ALU.subtract).then_inc(sems["lse_rel"], 1)
                dve.wait_ge(sems["att_weight"], p.count("att_weight"))
                Z = gat[:, :, 32:34]
                tt(Z, gat[:, :, 24:26], gat[:, :, 26:28], ALU.add)
                dve.drain()
                tt(Z, Z, gat[:, :, 28:30], ALU.add)
                dve.drain()
                tt(by_pattern(gat[:, :, 6:12]), by_pattern(gat[:, :, 6:12]), Z[:, :, None, :].to_broadcast((P, 2, 3, 2)),
                   ALU.mult)
                dve.drain()
                dve.reciprocal(gat[:, :, 36:42], gat[:, :, 6:12])
                dve.drain()
                tt(gat[:, :, 36:42], gat[:, :, 36:42], gat[:, :, 24:30], ALU.mult)
                dve.drain()
                for hh in range(2):
                    for g in range(3):
                        for t in range(NT):
                            c = 36 + 2 * g + t
                            r = ts(Pb[hh][:, g, t, :], Pb[hh][:, g, t, :], gat[:, hh, c:c + 1], None, ALU.mult)
                        r.then_inc(sems["att_prob"], 1)
                if pr == 0:
                    for j in range(3):
                        rotate(1, j)
                head_lo(pr, 0)
                if pr == 0:
                    rotate(1, 3)
                head_lo(pr, 1)
                if pr == 0:
                    rotate(1, 4)
                    rotate(1, 5)
            lo_parts(uT, (0, 1, 2, 3))
            dve.wait_ge(sems["gates_out"], p.count("gates_out", 8))
            for c in range(4):
                dve.wait_ge(sems["unit_done"], p.value("unit_done", b2 + 46 + 2 * c + 2))
                for q in range(2):
                    b = 4 + 2 * (c % 2) + q
                    tt(mixed[:, 2 * c + q, :], bank[b][:, 0:SEQ], gates[:, 2 * c + q, :], ALU.mult)\
                        .then_inc(sems[f"dve_read{b}"], 1)
            for half in range(2):
                dve.wait_ge(sems["unit_done"], p.value("unit_done", b2 + 54 + half + 1))
                for n in (2 * half, 2 * half + 1):
                    dve.drain()
                    tt(mixt, half2(n), gates[:, 8 + 2 * n:10 + 2 * n, :], ALU.mult).then_inc(sems[f"dve_read{n}"], 1)
                    dve.drain()
                    tt(mixed[:, 2 * n:2 * n + 2, :], mixed[:, 2 * n:2 * n + 2, :], mixt, ALU.add).then_inc(sems["mixed"], 1)
                dve.drain()
                for n in (2 * half, 2 * half + 1):
                    dve.wait_ge(sems["hi_part"], p.count("hi_part"))
                    k = slice(2 * n, 2 * n + 2)
                    tt(uT[1][:, k, :], mixed[:, k, :], uT[0][:, k, :].bitcast(F32), ALU.subtract).then_inc(sems["mixed_lo"], 1)

            def add_banks(u_last):
                for t in range(NT):
                    if t == 0:
                        dve.wait_ge(sems["first_rows"], p.count("first_rows"))
                    else:
                        dve.wait_ge(sems["unit_done"], p.value("unit_done", u_last + 1))
                    for h in range(2):
                        c = slice(h * 512, (h + 1) * 512)
                        r = tt(x[:, t, c], bank[2 * t + h][:, :], x[:, t, c], ALU.add)
                        r.then_inc(sems[("bank_added", "x_ready")[h]], 1)
            add_banks(b2 + 59)
            prenorm(x)
            lo_parts(uT, (4, 5, 6, 7))
            add_banks(ffn(b2 + 60))
            w = use_row()
            for t in range(NT):
                dve.wait_ge(sems["rms"], p.count("rms"))
                dve.reciprocal(st[:, t:t + 1], st[:, t:t + 1])
                dve.drain()
                r = stt(x[:, t, :], x[:, t, :], st[:, t:t + 1], w, ALU.mult, ALU.mult)
            r.then_inc(sems["out_ready"], 1)

        @block.tensor
        def _(pe):
            p = Prog(pe)
            state = {"unit": 0}
            last_reader = {}

            def acquire(b, reader):
                if reader is None:
                    return
                if b in last_reader:
                    pe.wait_ge(sems[last_reader[b]], p.count(last_reader[b]))
                last_reader[b] = f"{reader}_read{b}" if reader in ("act", "dve") else reader

            def mm3(o, l, r, start, stop):
                pe.matmul(o, l[0], r[0], start=start, stop=False)
                pe.matmul(o, l[0], r[1], start=False, stop=False)
                return pe.matmul(o, l[1], r[0], start=False, stop=stop)

            def unit():
                s = state["unit"] % RING
                pe.wait_ge(sems["w_lo"], p.count("w_lo"))
                state["unit"] += 1
                return whi[s], wlo[s]

            def proj_T(b, reader, src, arriving=()):
                acquire(b, reader)
                w = unit()
                for j in range(2):
                    for k in range(KT):
                        if arriving and j == 0 and k % 2 == 0 and arriving[k // 2] != b:
                            n = arriving[k // 2]
                            pe.wait_ge(sems[f"dve_read{n}"], p.count(f"dve_read{n}"))
                            del last_reader[n]
                        c = slice(k * 256 + j * P, k * 256 + (j + 1) * P)
                        r = mm3(bank[b][:, j * SEQ:(j + 1) * SEQ], (w[0][:, c], w[1][:, c]),
                                (src[0][:, k, :], src[1][:, k, :]), k == 0, k == KT - 1)
                r.then_inc(sems["unit_done"], 1)

            def proj_tok(b, reader, src):
                acquire(b, reader)
                w = unit()
                for t in range(NT):
                    for k in range(KT):
                        c = slice(k * 256, (k + 1) * 256)
                        tk = slice(t * P, (t + 1) * P)
                        r = mm3(bank[b][:, t * 256:(t + 1) * 256], (src[0][:, k, tk], src[1][:, k, tk]),
                                (w[0][:, c], w[1][:, c]), k == 0, k == KT - 1)
                r.then_inc(sems["unit_done"], 1)

            def proj_rows(src, k0, first, last):
                w = unit()
                for t in range(NT):
                    for h in range(2):
                        if first:
                            acquire(2 * t + h, "dve")
                        for k in range(2):
                            c = slice(k * D + h * 512, k * D + (h + 1) * 512)
                            tk = slice(t * P, (t + 1) * P)
                            r = mm3(bank[2 * t + h][:, :], (src[0][:, k0 + k, tk], src[1][:, k0 + k, tk]),
                                    (w[0][:, c], w[1][:, c]), first and k == 0, last and k == 1)
                        if last and t == 0 and h == 1:
                            r.then_inc(sems["first_rows"], 1)
                r.then_inc(sems["unit_done"], 1)

            def transposes(src, banks, ready, counts=(1, 1)):
                for t in range(NT):
                    pe.wait_ge(sems[ready], p.count(ready, counts[t]))
                    for n, b in enumerate(banks):
                        if t == 0:
                            acquire(b, "dve")
                        for k in range(2):
                            f = (2 * n + k) * P
                            r = pe.transpose(bank[b][:, k * SEQ + t * P:k * SEQ + (t + 1) * P], src[:, t, f:f + P], ident)
                        if t == NT - 1:
                            r.then_inc(sems[f"act_bank{b}"], 1)

            def split_ready(banks=(4, 5, 6, 7)):
                for b in banks:
                    pe.wait_ge(sems[f"dve_read{b}"], p.count(f"dve_read{b}"))
                    del last_reader[b]

            def ffn(src, between=None):
                def gate_up(q, arriving=(), between=None):
                    proj_T(4 + 2 * q, "silu_gate", src, arriving)
                    if between:
                        between()
                    proj_T(5 + 2 * q, "ff_product", src)

                def down(q, first=False, last=False):
                    pe.wait_ge(sems["h_lo"], p.count("h_lo"))
                    proj_rows(hT, 2 * q, first, last)
                gate_up(0, (4, 5, 6, 7))
                gate_up(1, between=between)
                down(0, first=True)
                for b in (4, 5):
                    del last_reader[b]
                gate_up(0)
                down(1)
                for b in range(4, 8):
                    del last_reader[b]
                with p.loop((CH - 3) // 2, {"w_lo": 6, "h_lo": 2}):
                    for q in range(2):
                        proj_T(6 - 2 * q, None, src)
                        proj_T(7 - 2 * q, None, src)
                        down(q)
                state["unit"] += 6 * ((CH - 3) // 2 - 1)
                down(0, last=True)

            pe.wait_ge(sems["ident_in"], 16)
            for L in range(DEPTH):
                transposes(ub, (4, 5, 6, 7), "u_ready")
                ffn(uT, lambda: transposes(ub, (0, 1, 2, 3), "u_ready"))
                transposes(ub, (4, 5, 6, 7), "u_ready")
                if L == 0:
                    pe.wait_ge(sems["cst_in"], 16)
                for j in range(6):
                    proj_T(j, "conv_in", uT, () if j else (4, 5, 6, 7))
                for b in (6, 7, 0, 1):
                    proj_T(b, "dve", uT)
                for j in range(4):
                    if j % 2 == 0:
                        pe.wait_ge(sems["squares"], p.count("squares"))
                    acquire(2 + j, "act")
                    pe.matmul(bank[2 + j][:, :], ones, arena[:, 512 * j:512 * (j + 1)], start=True, stop=True)\
                        .then_inc(sems[f"act_bank{2 + j}"], 1)
                proj_tok(6, "tok_out", uT)
                proj_tok(7, "tok_out", uT)
                pe.wait_ge(sems["ab_lo"], p.count("ab_lo"))
                acquire(0, "dve")
                for k in range(KT):
                    c = slice(k * 16, (k + 1) * 16)
                    r = mm3(bank[0][0:16, 0:SEQ], (ab[0][:, c], ab[1][:, c]), (uT[0][:, k, :], uT[1][:, k, :]),
                            k == 0, k == KT - 1)
                r.then_inc(sems["dve_bank0"], 1)

                def ret_scores(h):
                    b = 2 + h % 2
                    acquire(b, "dve")
                    for m in range(2):
                        r = pe.matmul(bank[b][:, m * 256:(m + 1) * 256], rkT[:, h, m * P:(m + 1) * P], rqT[:, h, :],
                                      start=True, stop=True)
                    r.then_inc(sems[f"dve_bank{b}"], 1)

                def ret_out(h):
                    pe.wait_ge(sems[f"dve_read{2 + h % 2}"], p.count(f"dve_read{2 + h % 2}"))
                    del last_reader[2 + h % 2]
                    for t in range(NT):
                        for m in range(2):
                            r = pe.matmul(bank[5 + t][:, h * P:(h + 1) * P], stb[h % 2][:, m, t * P:(t + 1) * P],
                                          rv[:, m, h * P:(h + 1) * P], start=(m == 0), stop=(m == 1))
                        if h == HEADS - 1:
                            r.then_inc(sems[f"dve_bank{5 + t}"], 1)
                    if h < 2:
                        r.then_inc(sems["st_used"], 1)

                proj_tok(1, "tok_out", uT)
                acquire(0, "dve")
                for t in range(NT):
                    r = pe.transpose(bank[0][:, t * 16:(t + 1) * 16], abT[0:16, t * P:(t + 1) * P], ident[0:16, 0:16])
                r.then_inc(sems["dve_bank0"], 1)
                pe.wait_ge(sems["rotated"], p.count("rotated", 4))
                ret_scores(0)
                ret_scores(1)
                proj_tok(4, "tok_out", uT)
                pe.wait_ge(sems["tok_out"], p.count("tok_out", 2))
                for b in (6, 7):
                    del last_reader[b]
                acquire(5, "dve")
                acquire(6, "dve")
                ret_out(0)
                ret_out(1)
                ret_scores(2)
                ret_scores(3)
                pe.wait_ge(sems["g_ready"], p.count("g_ready"))
                acquire(0, "dve")
                for c in range(2):
                    o = c * 16
                    pe.matmul(bank[0][:, o:o + 4], UI, gat[:, c, 0:4], start=True, stop=True)
                    pe.matmul(bank[0][:, o + 4:o + 8], LI, gat[:, c, 4:8], start=True, stop=True)
                    r = pe.matmul(bank[0][:, o + 8:o + 16], ones, gat[:, c, 0:8], start=True, stop=True)
                r.then_inc(sems["dve_bank0"], 1)
                proj_tok(7, "tok_out", uT)
                ret_out(2)
                ret_out(3)
                proj_tok(1, "tok_out", uT)
                pe.wait_ge(sems["tok_out"], p.count("tok_out", 3))
                for b in (1, 4, 7):
                    del last_reader[b]

                def memory_half(n):
                    v, half = n // 2, n % 2
                    b = (3, 7)[v % 2]
                    if half == 0:
                        acquire(b, "act")
                        unit()
                    slot = (state["unit"] - 1) % RING
                    w = whi[slot], wlo[slot]
                    for k in range(KT):
                        if v < 4:
                            c = slice(k * 256 + half * P, k * 256 + (half + 1) * P)
                            r = mm3(bank[b][:, half * SEQ:(half + 1) * SEQ], (w[0][:, c], w[1][:, c]),
                                    (mT[0][:, k, :], mT[1][:, k, :]), k == 0, k == KT - 1)
                        else:
                            c = slice(k * 256, (k + 1) * 256)
                            tk = slice(half * P, (half + 1) * P)
                            r = mm3(bank[b][:, half * 256:(half + 1) * 256], (mT[0][:, k, tk], mT[1][:, k, tk]),
                                    (w[0][:, c], w[1][:, c]), k == 0, k == KT - 1)
                    if half == 1:
                        r.then_inc(sems["unit_done"], 1)
                memory_half(0)
                memory_half(1)
                pe.wait_ge(sems["qk_unit"], p.count("qk_unit", 4))
                pe.wait_ge(sems["v_ready"], p.count("v_ready"))
                pe.wait_ge(sems["ret_done"], p.count("ret_done", 2))
                for j in range(4):
                    b = (0, 4, 5, 6)[j]
                    acquire(b, "act")
                    for h in range(HEADS):
                        tile = (4 if j < 2 else 8) + h
                        r = pe.transpose(bank[b][:, h * P:(h + 1) * P], cout[:, tile, (j % 2) * P:(j % 2 + 1) * P], ident)
                    r.then_inc(sems[f"act_bank{b}"], 1)
                for pair in range(2):
                    for s in range(2):
                        h = 2 * pair + s
                        acquire(4 * s, "dve")
                        for i in range(4):
                            c, dr = i % 2, i // 2
                            r = pe.matmul(bank[4 * s][:, i * P:(i + 1) * P],
                                          gat[:, c, 4 * dr + h:4 * dr + h + 1].to_broadcast((P, P)), (UI, LI)[dr],
                                          start=True, stop=True)
                        r.then_inc(sems[f"dve_bank{4 * s}"], 1)
                        acquire(4 * s + 1, "dve")
                        for i in range(4):
                            c = i % 2
                            ck = slice(c * P, (c + 1) * P)
                            r = pe.matmul(bank[4 * s + 1][:, i * P:(i + 1) * P], cout[:, 4 + h, ck],
                                          cout[:, (4 if i < 2 else 0) + h, ck], start=True, stop=True)
                        r.then_inc(sems[f"dve_bank{4 * s + 1}"], 1)
                    memory_half(2 + 8 * pair)
                    memory_half(3 + 8 * pair)
                    for s in range(2):
                        TT = G[s][5]
                        pe.wait_ge(sems["tt_first"], p.count("tt_first"))
                        acquire(4 * s + 2, "t_first")
                        for i in range(4):
                            r = pe.transpose(bank[4 * s + 2][:, i * P:(i + 1) * P], TT[:, i, :], ident)
                        r.then_inc(sems[f"act_bank{4 * s + 2}"], 1)
                        if s == 0:
                            memory_half(4 + 8 * pair)
                    for l in range(1, 7):
                        for s in range(2):
                            DT, LT, LM, PT, T, TT = G[s]
                            pe.wait_ge(sems["level"], p.count("level"))
                            acquire(4 * s, "act")
                            if l == 1:
                                pe.wait_ge(sems["t_first"], p.count("t_first"))
                            else:
                                pe.wait_ge(sems[f"dve_read{4 * s + 2}"], p.count(f"dve_read{4 * s + 2}"))
                            del last_reader[4 * s + 2]
                            for i in range(4):
                                r = pe.matmul(bank[4 * s][:, i * P:(i + 1) * P], LM[:, i, :], T[:, i, :], start=True, stop=True)
                            r.then_inc(sems[f"act_bank{4 * s}"], 1)
                        for s in range(2):
                            DT, LT, LM, PT, T, TT = G[s]
                            pe.wait_ge(sems[f"act_read{4 * s}"], p.count(f"act_read{4 * s}"))
                            del last_reader[4 * s]
                            if l < 6:
                                acquire(4 * s + 2, "dve")
                                for i in range(4):
                                    r = pe.matmul(bank[4 * s + 2][:, i * 64:(i + 1) * 64], TT[:, i, :],
                                                  blocks(DT[:, i, :], l, i // 2), start=True, stop=True)
                                    if i == 0:
                                        r.then_inc(sems["level_used"], 1)
                            acquire(4 * s + 1, "dve")
                            for i in range(4):
                                r = pe.matmul(bank[4 * s + 1][:, i * 64:(i + 1) * 64], DT[:, i, :],
                                              blocks(TT[:, i, :], l, 1 - i // 2), start=True, stop=True)
                            r.then_inc(sems[f"dve_bank{4 * s + 1}"], 1)
                    for s in range(2):
                        h = 2 * pair + s
                        DT, LT, LM, PT, T, TT = G[s]
                        hc = slice(h * P, (h + 1) * P)
                        pe.wait_ge(sems[f"dve_read{4 * s + 1}"], p.count(f"dve_read{4 * s + 1}"))
                        del last_reader[4 * s + 1]
                        acquire(4 * s, "dve")
                        for dr in range(2):
                            r = pe.matmul(bank[4 * s][:, dr * P:(dr + 1) * P], TT[:, 2 * dr + dr, :], vtok[:, dr, hc],
                                          start=True, stop=True)
                        r.then_inc(sems[f"dve_bank{4 * s}"], 1)
                    memory_half(5 + 8 * pair)
                    for s in range(2):
                        DT, LT, LM, PT, T, TT = G[s]
                        pe.wait_ge(sems[f"dve_read{4 * s}"], p.count(f"dve_read{4 * s}"))
                        del last_reader[4 * s]
                        acquire(4 * s + 1, "act")
                        for dr in range(2):
                            r = pe.matmul(bank[4 * s + 1][:, dr * P:(dr + 1) * P], LT[:, dr, :], T[:, 2 * dr + dr, :],
                                          start=True, stop=True)
                        r.then_inc(sems[f"act_bank{4 * s + 1}"], 1)
                    if pair == 0:
                        memory_half(6)
                    for s in range(2):
                        h = 2 * pair + s
                        DT, LT, LM, PT, T, TT = G[s]
                        pe.wait_ge(sems[f"act_read{4 * s + 1}"], p.count(f"act_read{4 * s + 1}"))
                        del last_reader[4 * s + 1]
                        acquire(4 * s + 2, "dve")
                        for q in range(2):
                            for dr in range(2):
                                cB = slice((1 - dr) * P, (2 - dr) * P)
                                r = pe.matmul(bank[4 * s + 2][:, (2 * q + dr) * P:(2 * q + dr + 1) * P],
                                              cout[:, (4, 0)[q] + h, cB], LM[:, dr, :], start=True, stop=True)
                        r.then_inc(sems[f"dve_bank{4 * s + 2}"], 1)
                    if pair == 0:
                        memory_half(7)
                    for s in range(2):
                        DT, LT, LM, PT, T, TT = G[s]
                        pe.wait_ge(sems["rest"], p.count("rest"))
                        acquire(4 * s + 1, "dve")
                        for dr in range(2):
                            r = pe.matmul(bank[4 * s + 1][:, dr * P:(dr + 1) * P], TT[:, 2 * dr + (1 - dr), :],
                                          LT[:, 2 + dr, :], start=True, stop=True)
                        r.then_inc(sems[f"dve_bank{4 * s + 1}"], 1)
                    if pair == 0:
                        memory_half(8)
                    for s in range(2):
                        DT, LT, LM, PT, T, TT = G[s]
                        pe.wait_ge(sems[f"dve_read{4 * s + 1}"], p.count(f"dve_read{4 * s + 1}"))
                        del last_reader[4 * s + 1]
                        acquire(4 * s, "dve")
                        for c in range(2):
                            for dr in range(2):
                                r = pe.matmul(bank[4 * s][:, c * P:(c + 1) * P], PT[:, 2 * dr + c, :], T[:, 2 * dr + c, :],
                                              start=(dr == 0), stop=(dr == 1))
                        r.then_inc(sems[f"dve_bank{4 * s}"], 1)
                    if pair == 0:
                        memory_half(9)
                    else:
                        memory_half(14)
                        memory_half(15)
                transposes(osb, (4, 5, 6, 7), "mix_ready")
                for j in range(4):
                    pe.wait_ge(sems[f"dve_read{4 + j}"], p.count(f"dve_read{4 + j}"))
                    del last_reader[4 + j]
                    proj_rows(uT, 2 * j, j == 0, j == 3)
                transposes(ub, (4, 5, 6, 7), "u_ready")

                def xscores(h):
                    pe.wait_ge(sems[f"act_read{h}"], p.count(f"act_read{h}"))
                    del last_reader[h]
                    acquire(4 + h, "xexp")
                    for t in range(NT):
                        for d in range(2):
                            r = pe.matmul(bank[4 + h][:, t * 256:(t + 1) * 256], qx[:, 2 * h + d, t * P:(t + 1) * P],
                                          kx[:, 2 * h + d, :], start=(d == 0), stop=(d == 1))
                    r.then_inc(sems[f"dve_bank{4 + h}"], 1)

                def xprobs_T(h):
                    pe.wait_ge(sems["xprob"], p.count("xprob"))
                    acquire(h, "act")
                    for m in range(2):
                        for t in range(NT):
                            r = pe.transpose(bank[h][:, m * SEQ + t * P:m * SEQ + (t + 1) * P],
                                             px[h % 2][:, t, m * P:(m + 1) * P], ident)
                    r.then_inc(sems[f"act_bank{h}"], 1)

                def xhead(h):
                    pe.wait_ge(sems[f"act_read{h}"], p.count(f"act_read{h}"))
                    del last_reader[h]
                    acquire(4 + h, "dve")
                    for e in range(2):
                        for m in range(2):
                            r = pe.matmul(bank[4 + h][:, e * SEQ:(e + 1) * SEQ], vx[h][:, m, e * P:(e + 1) * P],
                                          pxT[h % 2][:, m, :], start=(m == 0), stop=(m == 1))
                    r.then_inc(sems[f"act_bank{4 + h}"], 1)

                proj_T(0, "act", uT, (4, 5, 6, 7))
                proj_T(1, "act", uT)
                xscores(0)
                proj_T(2, "act", uT)
                xscores(1)
                xprobs_T(0)
                proj_T(3, "act", uT)
                xscores(2)
                xhead(0)
                xprobs_T(1)
                xscores(3)
                xhead(1)
                for h in (2, 3):
                    xprobs_T(h)
                    xhead(h)
                for j in range(4):
                    pe.wait_ge(sems[f"dve_read{4 + j}"], p.count(f"dve_read{4 + j}"))
                    del last_reader[4 + j]
                    proj_rows(uT, 2 * j, j == 0, j == 3)
                transposes(ub, (4, 5, 6, 7), "u_ready")
                ffn(uT)

            transposes(ub, (4, 5, 6, 7), "u_ready")
            proj_T(conv_bank[0], "conv_in", uT, (4, 5, 6, 7))
            proj_T(conv_bank[1], "conv_in", uT)
            pe.wait_ge(sems["wdt_lo"], p.count("wdt_lo"))
            acquire(0, "dve")
            for k in range(KT):
                c = slice(k * 32, (k + 1) * 32)
                r = mm3(bank[0][0:32, 0:SEQ], (wdt[0][:, c], wdt[1][:, c]), (uT[0][:, k, :], uT[1][:, k, :]),
                        k == 0, k == KT - 1)
            r.then_inc(sems["dve_bank0"], 1)
            proj_T(conv_bank[2], "conv_in", uT)
            acquire(0, "dve")
            for t in range(NT):
                r = pe.transpose(bank[0][:, t * 32:(t + 1) * 32], dtT[0:32, t * P:(t + 1) * P], ident[0:32, 0:32])
            r.then_inc(sems["dve_bank0"], 1)
            for g in range(SSM_GROUPS):
                for j in range(2):
                    proj_tok(z_bank[j], "tok_out", uT)
                if g == 0:
                    pe.wait_ge(sems["g_ready"], p.count("g_ready"))
                    acquire(1, "dve")
                    for c in range(2):
                        pe.matmul(bank[1][:, c * 64:c * 64 + 32], UI, gs[:, c, 32:64], start=True, stop=True)
                        r = pe.matmul(bank[1][:, c * 64 + 32:c * 64 + 64], ones, gs[:, c, 32:64], start=True, stop=True)
                    r.then_inc(sems["dve_bank1"], 1)
                if g == 2:
                    transposes(ysb, (0, 1, 4, 5), "y_ready", (3, 1))
                pe.wait_ge(sems["conv_silu"], p.count("conv_silu", 2))
                acquire(0, "dve")
                for c in range(2):
                    ck = slice(c * P, (c + 1) * P)
                    pe.matmul(bank[0][:, ck], cout2[:, 0, ck], cout2[:, 1, ck], start=True, stop=True)
                pe.transpose(bank[0][:, 256:384], cout2[:, 0, 0:P], ident).then_inc(sems["dve_bank0"], 1)
                for c in range(2):
                    b = (1, 7)[c]
                    acquire(b, "xs_out")
                    for i in range(4):
                        r = pe.transpose(bank[b][:, i * P:(i + 1) * P], cout2[:, 2 + i, c * P:(c + 1) * P], ident)
                    r.then_inc(sems[f"act_bank{b}"], 1)

                def row_sums(hp):
                    b = 4 + hp % 2
                    acquire(b, "dve")
                    for i in range(4):
                        c, h = i % 2, 8 * g + 2 * hp + i // 2
                        r = pe.matmul(bank[b][:, i * P:(i + 1) * P], gs[:, c, 32 + h:33 + h].to_broadcast((P, P)), UI,
                                      start=True, stop=True)
                    r.then_inc(sems[f"dve_bank{b}"], 1)
                proj_T(conv_bank[0], "conv_in" if g < SSM_GROUPS - 1 else "dve", uT)
                row_sums(0)
                row_sums(1)
                pe.wait_ge(sems["x_dt"], p.count("x_dt"))
                acquire(0, "act")
                pe.matmul(bank[0][:, :], btok, xdec, start=True, stop=True).then_inc(sems["act_bank0"], 1)
                proj_T(conv_bank[1], "conv_in" if g < SSM_GROUPS - 1 else "dve", uT)
                acquire(0, "dve")
                pe.matmul(bank[0][:, :], cout2[:, 1, P:2 * P], Ssb, start=True, stop=True).then_inc(sems["dve_bank0"], 1)
                acquire(1, "dve")
                acquire(7, "dve")
                for hp in range(4):
                    pe.wait_ge(sems["m_ready"], p.count("m_ready"))
                    for c in range(2):
                        for q in range(2):
                            h = 2 * hp + q
                            r = pe.matmul(bank[(1, 7)[c]][:, h * 64:(h + 1) * 64], Eb[hp % 2][:, 2 * q + c, :],
                                          xdt[:, c, h * 64:(h + 1) * 64], start=True, stop=True)
                        if hp == 3:
                            r.then_inc(sems[f"dve_bank{(1, 7)[c]}"], 1)
                    if hp < 3:
                        r.then_inc(sems["m_used"], 1)
                    if hp + 2 < 4:
                        row_sums(hp + 2)
                if g < SSM_GROUPS - 1:
                    proj_T(conv_bank[2], "conv_in", uT)

            def scores(hh):
                for g in range(3):
                    b = 3 * hh + g
                    acquire(b, "dve")
                    for t in range(NT):
                        r = pe.matmul(bank[b][:, t * SEQ:(t + 1) * SEQ], qa[:, g, hh, t * P:(t + 1) * P],
                                      ka[:, g, hh, :], start=True, stop=True)
                    r.then_inc(sems[f"dve_bank{b}"], 1)

            def probs_T(hh):
                for g in range(3):
                    pe.wait_ge(sems["att_prob"], p.count("att_prob"))
                    b = (6, 7, 0)[g]
                    acquire(b, "probs_T")
                    for m in range(2):
                        for t in range(NT):
                            r = pe.transpose(bank[b][:, m * SEQ + t * P:m * SEQ + (t + 1) * P],
                                             Pb[hh][:, g, t, m * P:(m + 1) * P], ident)
                    r.then_inc(sems[f"act_bank{b}"], 1)

            def head_out(hh):
                pe.wait_ge(sems["probs_T"], p.count("probs_T", 3))
                for b in (6, 7, 0):
                    del last_reader[b]
                acquire(3, "dve")
                for g in range(3):
                    for m in range(2):
                        r = pe.matmul(bank[3][:, 0:SEQ], va[:, g, m, hh * P:(hh + 1) * P], PTb[:, g, m, :],
                                      start=(g == 0 and m == 0), stop=(g == 2 and m == 1))
                r.then_inc(sems["act_bank3"], 1)

            for j in range(2, 6):
                proj_T(qk_bank[0][j], "dve", uT)
            for pr in range(2):
                proj_tok(6, "tok_out", uT)
                pe.wait_ge(sems["rotated"], p.count("rotated", 6))
                scores(0)
                scores(1)
                proj_tok(7, "tok_out", uT)
                proj_tok(6, "tok_out", uT)
                for n in range(4):
                    if n == 2:
                        pe.wait_ge(sems["tok_out"], p.count("tok_out", 2))
                        for b in (6, 7):
                            del last_reader[b]
                        probs_T(0)
                    if n == 3:
                        head_out(0)
                        probs_T(1)
                    proj_T(gate_bank[n] if pr else qk_bank[1][n], "gates_out" if pr else "dve", uT)
                head_out(1)
                for n in range(4, 8 if pr else 6):
                    proj_T(gate_bank[n % 4] if pr else qk_bank[1][n], "gates_out" if pr else "dve", uT)
            pe.wait_ge(sems["gates_out"], p.count("gates_out", 4))
            for b in gate_bank:
                del last_reader[b]
            transposes(ysb, (0, 1, 2, 3), "y_ready", (3, 1))
            for c in range(4):
                for half in range(2):
                    if c == 0 and half == 1:
                        split_ready((0, 1, 2, 3))
                    w = unit()
                    for q in range(2):
                        b = 4 + 2 * (c % 2) + q
                        if half == 0:
                            acquire(b, "dve")
                        src = (mT, uT)[half]
                        for k in range(KT):
                            cc = slice(k * 256 + q * P, k * 256 + (q + 1) * P)
                            r = mm3(bank[b][:, 0:SEQ], (w[0][:, cc], w[1][:, cc]), (src[0][:, k, :], src[1][:, k, :]),
                                    half == 0 and k == 0, half == 1 and k == KT - 1)
                    r.then_inc(sems["unit_done"], 1)
            for half in range(2):
                w = unit()
                for q in range(4):
                    b = 2 * half + q // 2
                    if q % 2 == 0:
                        acquire(b, "dve")
                    for k in range(4):
                        cc = slice(k * 512 + q * P, k * 512 + (q + 1) * P)
                        r = mm3(bank[b][:, (q % 2) * SEQ:(q % 2 + 1) * SEQ], (w[0][:, cc], w[1][:, cc]),
                                (hT[0][:, k, :], hT[1][:, k, :]), k == 0, k == 3)
                r.then_inc(sems["unit_done"], 1)
            for j in range(4):
                pe.wait_ge(sems["mixed_lo"], p.count("mixed_lo"))
                proj_rows(uT, 2 * j, j == 0, j == 3)
            for b in range(4):
                del last_reader[b]
            transposes(ub, (4, 5, 6, 7), "u_ready")
            ffn(uT)


def pack(v):
    f = {k: np.asarray(t) for k, t in v.items()}
    w = np.empty((N_UNITS, P, UNIT), np.float32)
    n = 0

    def cols(m):
        nonlocal n
        K, C = m.shape
        u = m.reshape(K // D, KT, P, C // 256, 256).transpose(3, 0, 2, 1, 4).reshape(-1, P, UNIT)
        w[n:n + len(u)] = u
        n += len(u)

    def rws(m):
        nonlocal n
        u = m.reshape(-1, 2, P, D).transpose(0, 2, 1, 3).reshape(-1, P, UNIT)
        w[n:n + len(u)] = u
        n += len(u)

    def ffn(g, u, d):
        cols(g[:, 0:256])
        cols(u[:, 0:256])
        for c in range(1, CH):
            cols(g[:, c * 256:(c + 1) * 256])
            cols(u[:, c * 256:(c + 1) * 256])
            rws(d[(c - 1) * 256:c * 256])
        rws(d[(CH - 1) * 256:])

    small = np.zeros((DEPTH, P, 340), np.float32)
    for l in range(DEPTH):
        ffn(f["ffn1_gate"][l], f["ffn1_up"][l], f["ffn1_down"][l])
        wi = f["w_in"][l]
        cols(wi[:, 2048:3584])
        cols(wi[:, 0:2048])
        cols(wi[:, 3584:4096])
        cols(f["xattn_k"][l])
        cols(f["xattn_v"][l])
        rws(f["w_out"][l])
        cols(f["xattn_q"][l])
        rws(f["xattn_o"][l])
        ffn(f["ffn2_gate"][l], f["ffn2_up"][l], f["ffn2_down"][l])
        s = small[l]
        s[:, 0:8] = f["ret_log_gamma"][l].reshape(1, 8)
        s[:, 8:16] = f["gdn_a_log"][l].reshape(1, 8)
        s[:, 16:24] = f["gdn_dt_bias"][l].reshape(1, 8)
        s[:, 24:152] = f["gdn_norm"][l].reshape(1, P)
        s[:, 152:212] = f["gdn_conv"][l].reshape(5, 12, P).transpose(2, 1, 0).reshape(P, 60)
        s[:, 212:340] = wi[:, 4096:4112].reshape(KT, P, 16).transpose(1, 0, 2).reshape(P, 128)
    rows = []
    for l in range(DEPTH):
        pre, post = f["norm_pre"][l], f["norm_post"][l]
        rows += [pre[0], f["mem_norm"][l], post[0], pre[1], post[1], pre[2], post[2], pre[3], post[3]]
    sn = f["ssm_norm_2"][0]
    rows += [f["norm_mix_2"][0], sn[0:D], sn[D:], f["norm_ffn_2"][0], f["norm_final_2"]]

    def att(m):
        nonlocal n
        w[n:n + 2] = m.reshape(4, P, 2, 512).transpose(2, 1, 0, 3).reshape(2, P, UNIT)
        n += 2
    small2 = second_pack(f, cols, rws, ffn, att)
    assert n == N_UNITS
    tiled = lambda m: np.ascontiguousarray(m.reshape(NT, P, D).transpose(1, 0, 2))
    arrays = {
        "w": w, "small": small, "rows": np.stack(rows), "x": tiled(f["x"][0]), "mem": tiled(f["mem"][0]),
        "pos": np.ascontiguousarray(f["positions"][0:1]), "cst": shape_constants(), "lvl": level_masks(),
        "small2": small2, "rope": rope_tables(), "amask": attention_masks(),
    }
    return arrays


def second_pack(f, cols, rws, ffn, att):
    wi = f["w_in_2"][0]
    xbc, z = 2048, 0
    for g in range(SSM_GROUPS):
        bcx = xbc + 2048 + g * P
        cols(np.concatenate([wi[:, bcx:bcx + P], wi[:, bcx + 512:bcx + 512 + P]], axis=1))
        cols(wi[:, xbc + g * 512:xbc + (g + 1) * 512])
        cols(wi[:, z + g * 512:z + (g + 1) * 512])
    qkv = 5120 + SSM_HEADS
    for pr in range(2):
        for kind, g in [(kind, g) for g in range(3) for kind in range(2)] + [(2, g) for g in range(3)]:
            o = qkv + kind * 1536 + (4 * g + 2 * pr) * P
            cols(wi[:, o:o + 256])
    cols(wi[:, qkv + 4608:])
    cols(f["w_ssm_out_2"][0])
    att(f["w_att_out_2"][0])
    rws(f["w_mix_out_2"][0])
    ffn(f["w_ffn_gate_2"][0], f["w_ffn_up_2"][0], f["w_ffn_down_2"][0])
    s = np.zeros((P, 488), np.float32)
    s[:, 0:32] = f["dt_bias_2"][0].reshape(1, 32)
    s[:, 32:64] = f["a_log_2"][0].reshape(1, 32)
    s[:, 64:96] = f["d_skip_2"][0].reshape(1, 32)
    order = [t for g in range(SSM_GROUPS) for t in [16 + g, 20 + g] + [4 * g + i for i in range(4)]]
    s[:, 96:192] = f["conv_w_2"][0].reshape(4, 24, P)[:, order].transpose(2, 1, 0).reshape(P, 96)
    s[:, 192:216] = f["conv_b_2"][0].reshape(24, P)[order].T
    s[:, 216:232] = f["b_gate_2"][0].reshape(16, P).T
    s[:, 232:488] = wi[:, 5120:5120 + SSM_HEADS].reshape(KT, P, 32).transpose(1, 0, 2).reshape(P, 256)
    return s


def kernel(**inputs):
    import concourse.bacc as bacc
    from concourse.bass_utils import run_bass_kernel_spmd as run

    nc = bacc.Bacc("TRN2", target_bir_lowering=False, num_devices=1)
    arrays = {f"in_{k}": v for k, v in pack(inputs).items()}
    a = {k[3:]: nc.dram_tensor(k, v.shape, mybir.dt.from_np(v.dtype), kind="ExternalInput").ap() for k, v in arrays.items()}
    out = nc.dram_tensor("out", (1, SEQ, D), F32, kind="ExternalOutput").ap()
    build(nc, a, out)
    return run(nc, [arrays], core_ids=[0]).results[0]["out"]
```
